# Optimizing a Trainium2 kernel written in Bass

```python
import jax, jax.numpy as jnp
from jax import lax
import numpy as np

D_MODEL = 2048
BATCH = 1
SEQ = 256
DEPTH = 1

CHUNK = 64
Q_BLOCK = 128
N_MEM = 256
EPS = 1e-6
MLA_HEADS = 16
Q_LORA_RANK = 512
KV_LORA_RANK = 512
QK_NOPE_DIM = 128
QK_ROPE_DIM = 64
V_HEAD_DIM = 128
ROPE_BASE = 10000.0
MLA_WIDTH = MLA_HEADS * V_HEAD_DIM
MLSTM_HEADS = 8
MLSTM_QK_DIM = 128
MLSTM_V_DIM = 256
MLSTM_CONV = 4
MLSTM_QK_WIDTH = MLSTM_HEADS * MLSTM_QK_DIM
MLSTM_V_WIDTH = MLSTM_HEADS * MLSTM_V_DIM
CROSS_HEADS = 4
CROSS_HEAD_DIM = 128
CROSS_WIDTH = CROSS_HEADS * CROSS_HEAD_DIM
D_FF = 5632
FFN_CONV = 3
IN_SPLITS = (Q_LORA_RANK, KV_LORA_RANK, QK_ROPE_DIM,
             MLSTM_QK_WIDTH, MLSTM_QK_WIDTH, MLSTM_V_WIDTH, MLSTM_HEADS, MLSTM_HEADS, MLSTM_V_WIDTH,
             D_MODEL, D_MODEL)
IN_WIDTH = (Q_LORA_RANK + KV_LORA_RANK + QK_ROPE_DIM + 2 * MLSTM_QK_WIDTH + MLSTM_V_WIDTH
            + 2 * MLSTM_HEADS + MLSTM_V_WIDTH + 2 * D_MODEL)

kernel_name = "hybrid_mla_mlstm_gated_streaming_layer"

def rms_norm(x, g):
    xf = x.astype(jnp.float32)
    y = xf * lax.rsqrt(jnp.mean(xf * xf, axis=-1, keepdims=True) + EPS)
    return (y * g.astype(jnp.float32)).astype(x.dtype)

def causal_dwconv(x, w):
    k_width, s = w.shape[0], x.shape[1]
    xp = jnp.pad(x, ((0, 0), (k_width - 1, 0), (0, 0)))
    return sum(xp[:, j:j + s] * w[j] for j in range(k_width))

def rope_tables(positions):
    inv_freq = ROPE_BASE ** (-jnp.arange(0, QK_ROPE_DIM, 2, dtype=jnp.float32) / QK_ROPE_DIM)
    ang = positions.astype(jnp.float32)[..., None] * inv_freq
    return jnp.cos(ang), jnp.sin(ang)

def apply_rope(x, cos, sin):
    half = x.shape[-1] // 2
    x1, x2 = x[..., :half], x[..., half:]
    return jnp.concatenate([x1 * cos - x2 * sin, x2 * cos + x1 * sin], axis=-1).astype(x.dtype)

def mla_attention(z_qa, z_kv, z_kpe, cos, sin, g_qa, w_qb, g_kva, w_kvb,
                  g_qn_nope, g_qn_pe, g_kn_nope, g_kn_pe):
    b, s, _ = z_qa.shape
    q = (rms_norm(z_qa, g_qa) @ w_qb).reshape(b, s, MLA_HEADS, QK_NOPE_DIM + QK_ROPE_DIM)
    kv = (rms_norm(z_kv, g_kva) @ w_kvb).reshape(b, s, MLA_HEADS, QK_NOPE_DIM + V_HEAD_DIM)
    q_nope = rms_norm(q[..., :QK_NOPE_DIM], g_qn_nope)
    q_pe = apply_rope(rms_norm(q[..., QK_NOPE_DIM:], g_qn_pe), cos[:, :, None], sin[:, :, None])
    k_nope = rms_norm(kv[..., :QK_NOPE_DIM], g_kn_nope)
    v = kv[..., QK_NOPE_DIM:]
    k_pe = apply_rope(rms_norm(z_kpe, g_kn_pe), cos, sin)
    scale = (QK_NOPE_DIM + QK_ROPE_DIM) ** -0.5
    outs = []
    for j in range(s // Q_BLOCK):
        q0, q1 = j * Q_BLOCK, (j + 1) * Q_BLOCK
        k_end = q1
        sc = (jnp.einsum('bqhd,bkhd->bhqk', q_nope[:, q0:q1], k_nope[:, :k_end])
              + jnp.einsum('bqhr,bkr->bhqk', q_pe[:, q0:q1], k_pe[:, :k_end])).astype(jnp.float32) * scale
        q_chunk = (q0 + jnp.arange(Q_BLOCK)) // CHUNK
        k_chunk = jnp.arange(k_end) // CHUNK
        sc = jnp.where(k_chunk[None, :] <= q_chunk[:, None], sc, -jnp.inf)
        p = jax.nn.softmax(sc, axis=-1).astype(v.dtype)
        outs.append(jnp.einsum('bhqk,bkhd->bqhd', p, v[:, :k_end]))
    return jnp.concatenate(outs, axis=1).reshape(b, s, MLA_WIDTH)

def mlstm(zq, zk, zv, zi, zf, zo, conv_qk, b_if, g_hnorm):
    b, s, _ = zq.shape
    h_, dk, dv, l_ = MLSTM_HEADS, MLSTM_QK_DIM, MLSTM_V_DIM, CHUNK
    nc = s // l_
    qk = jax.nn.silu(causal_dwconv(jnp.concatenate([zq, zk], axis=-1), conv_qk))

    def to_chunks(t, d):
        return t.astype(jnp.float32).reshape(b, nc, l_, h_, d).transpose(1, 0, 3, 2, 4)

    q = to_chunks(qk[..., :MLSTM_QK_WIDTH], dk) * (dk ** -0.5)
    k = to_chunks(qk[..., MLSTM_QK_WIDTH:], dk)
    v = to_chunks(zv, dv)
    gates = (jnp.concatenate([zi, zf], axis=-1) + b_if).astype(jnp.float32)

    def gate_chunks(t):
        return t.reshape(b, nc, l_, h_).transpose(1, 0, 3, 2)

    log_i = gate_chunks(gates[..., :h_])
    bcum = jnp.cumsum(gate_chunks(jax.nn.log_sigmoid(gates[..., h_:])), axis=-1)
    causal = jnp.tril(jnp.ones((l_, l_), dtype=bool))

    def step(carry, inp):
        c_mat, n_vec, m = carry
        qc, kc, vc, bc, ic = inp
        logw = jnp.where(causal, bc[..., :, None] - bc[..., None, :] + ic[..., None, :], -jnp.inf)
        inter = bc + m[..., None]
        m_t = jnp.maximum(inter, jnp.max(logw, axis=-1))
        w_intra = jnp.exp(logw - m_t[..., None])
        w_inter = jnp.exp(inter - m_t)
        sc = jnp.einsum('bhtd,bhsd->bhts', qc, kc) * w_intra
        num = w_inter[..., None] * jnp.einsum('bhtd,bhde->bhte', qc, c_mat) + jnp.einsum('bhts,bhse->bhte', sc, vc)
        den = w_inter * jnp.einsum('bhtd,bhd->bht', qc, n_vec) + jnp.sum(sc, axis=-1)
        h = num / jnp.maximum(jnp.abs(den), jnp.exp(-m_t))[..., None]
        b_last = bc[..., -1]
        logu = b_last[..., None] - bc + ic
        m_new = jnp.maximum(b_last + m, jnp.max(logu, axis=-1))
        decay = jnp.exp(b_last + m - m_new)
        u = jnp.exp(logu - m_new[..., None])
        c_mat = decay[..., None, None] * c_mat + jnp.einsum('bhs,bhsd,bhse->bhde', u, kc, vc)
        n_vec = decay[..., None] * n_vec + jnp.einsum('bhs,bhsd->bhd', u, kc)
        return (c_mat, n_vec, m_new), h

    init = (jnp.zeros((b, h_, dk, dv), jnp.float32), jnp.zeros((b, h_, dk), jnp.float32),
            jnp.zeros((b, h_), jnp.float32))
    _, h = lax.scan(step, init, (q, k, v, bcum, log_i))
    h = h.transpose(1, 0, 3, 2, 4).reshape(b, s, h_, dv)
    h = rms_norm(h, g_hnorm).reshape(b, s, MLSTM_V_WIDTH).astype(zq.dtype)
    return h * jax.nn.sigmoid(zo)

def cross_attend(u, mm, wq_c, wk_c, wv_c, g_cq, g_ck, wo_c):
    b, s, _ = u.shape
    n_mem = mm.shape[1]
    q = rms_norm((u @ wq_c).reshape(b, s, CROSS_HEADS, CROSS_HEAD_DIM), g_cq)
    k = rms_norm((mm @ wk_c).reshape(b, n_mem, CROSS_HEADS, CROSS_HEAD_DIM), g_ck)
    v = (mm @ wv_c).reshape(b, n_mem, CROSS_HEADS, CROSS_HEAD_DIM)
    sc = jnp.einsum('bqhd,bkhd->bhqk', q, k).astype(jnp.float32) * (CROSS_HEAD_DIM ** -0.5)
    p = jax.nn.softmax(sc, axis=-1).astype(v.dtype)
    o = jnp.einsum('bhqk,bkhd->bqhd', p, v).reshape(b, s, CROSS_WIDTH)
    return o @ wo_c

def conv_glu_ffn(u, w_up, conv_ffn, b_conv_ffn, w_down):
    h = causal_dwconv(u @ w_up, conv_ffn) + b_conv_ffn
    return (jax.nn.silu(h[..., :D_FF]) * h[..., D_FF:]) @ w_down

def hybrid_layer(x, mem, cos, sin, g_mix, w_in, g_qa, w_qb, g_kva, w_kvb, g_qn_nope, g_qn_pe,
                 g_kn_nope, g_kn_pe, conv_qk, b_if, g_hnorm, p_a, p_b, w_out, g_cross, g_mem,
                 wq_c, wk_c, wv_c, g_cq, g_ck, wo_c, g_ffn, w_up, conv_ffn, b_conv_ffn, w_down):
    split_points = [int(p) for p in np.cumsum(IN_SPLITS)[:-1]]
    z = rms_norm(x, g_mix) @ w_in
    z_qa, z_kv, z_kpe, zq, zk, zv, zi, zf, zo, gate_a, gate_b = jnp.split(z, split_points, axis=-1)
    y_a = mla_attention(z_qa, z_kv, z_kpe, cos, sin, g_qa, w_qb, g_kva, w_kvb,
                        g_qn_nope, g_qn_pe, g_kn_nope, g_kn_pe)
    y_b = mlstm(zq, zk, zv, zi, zf, zo, conv_qk, b_if, g_hnorm)
    merged = jax.nn.sigmoid(gate_a) * (y_a @ p_a) + jax.nn.sigmoid(gate_b) * (y_b @ p_b)
    x = x + merged @ w_out
    x = x + cross_attend(rms_norm(x, g_cross), rms_norm(mem, g_mem), wq_c, wk_c, wv_c, g_cq, g_ck, wo_c)
    x = x + conv_glu_ffn(rms_norm(x, g_ffn), w_up, conv_ffn, b_conv_ffn, w_down)
    return x

def setup_inputs(seed: int = 0) -> dict:
    key = jax.random.key(seed)
    ks = iter(jax.random.split(key, 64))
    f32 = jnp.float32

    def w(shape, fan_in):
        return jax.random.normal(next(ks), (DEPTH,) + shape, f32) * (fan_in ** -0.5)

    def gain(shape):
        return 1.0 + 0.05 * jax.random.normal(next(ks), (DEPTH,) + shape, f32)

    x = jax.random.normal(next(ks), (BATCH, SEQ, D_MODEL), f32)
    mem = jax.random.normal(next(ks), (BATCH, N_MEM, D_MODEL), f32)
    offset = jax.random.randint(next(ks), (BATCH, 1), 0, 4096, dtype=jnp.int32)
    positions = (offset + jnp.arange(SEQ, dtype=jnp.int32)[None, :]).astype(jnp.int32)
    b_i = 0.1 * jax.random.normal(next(ks), (DEPTH, MLSTM_HEADS), f32)
    b_f = jnp.linspace(3.0, 6.0, MLSTM_HEADS, dtype=f32)[None, :] + 0.1 * jax.random.normal(next(ks), (DEPTH, MLSTM_HEADS), f32)
    return {
        "x": x,
        "mem": mem,
        "positions": positions,
        "g_mix": gain((D_MODEL,)),
        "w_in": w((D_MODEL, IN_WIDTH), D_MODEL),
        "g_qa": gain((Q_LORA_RANK,)),
        "w_qb": w((Q_LORA_RANK, MLA_HEADS * (QK_NOPE_DIM + QK_ROPE_DIM)), Q_LORA_RANK),
        "g_kva": gain((KV_LORA_RANK,)),
        "w_kvb": w((KV_LORA_RANK, MLA_HEADS * (QK_NOPE_DIM + V_HEAD_DIM)), KV_LORA_RANK),
        "g_qn_nope": gain((QK_NOPE_DIM,)),
        "g_qn_pe": gain((QK_ROPE_DIM,)),
        "g_kn_nope": gain((QK_NOPE_DIM,)),
        "g_kn_pe": gain((QK_ROPE_DIM,)),
        "conv_qk": w((MLSTM_CONV, 2 * MLSTM_QK_WIDTH), MLSTM_CONV),
        "b_if": jnp.concatenate([b_i, b_f], axis=-1),
        "g_hnorm": gain((MLSTM_HEADS, MLSTM_V_DIM)),
        "p_a": w((MLA_WIDTH, D_MODEL), MLA_WIDTH),
        "p_b": w((MLSTM_V_WIDTH, D_MODEL), MLSTM_V_WIDTH),
        "w_out": w((D_MODEL, D_MODEL), D_MODEL),
        "g_cross": gain((D_MODEL,)),
        "g_mem": gain((D_MODEL,)),
        "wq_c": w((D_MODEL, CROSS_WIDTH), D_MODEL),
        "wk_c": w((D_MODEL, CROSS_WIDTH), D_MODEL),
        "wv_c": w((D_MODEL, CROSS_WIDTH), D_MODEL),
        "g_cq": gain((CROSS_HEAD_DIM,)),
        "g_ck": gain((CROSS_HEAD_DIM,)),
        "wo_c": w((CROSS_WIDTH, D_MODEL), CROSS_WIDTH),
        "g_ffn": gain((D_MODEL,)),
        "w_up": w((D_MODEL, 2 * D_FF), D_MODEL),
        "conv_ffn": w((FFN_CONV, 2 * D_FF), FFN_CONV),
        "b_conv_ffn": 0.01 * jax.random.normal(next(ks), (DEPTH, 2 * D_FF), f32),
        "w_down": w((D_FF, D_MODEL), D_FF),
    }

def reference(x, mem, positions, g_mix, w_in, g_qa, w_qb, g_kva, w_kvb, g_qn_nope, g_qn_pe,
              g_kn_nope, g_kn_pe, conv_qk, b_if, g_hnorm, p_a, p_b, w_out, g_cross, g_mem,
              wq_c, wk_c, wv_c, g_cq, g_ck, wo_c, g_ffn, w_up, conv_ffn, b_conv_ffn, w_down):
    cos, sin = rope_tables(positions)
    for l in range(DEPTH):
        x = hybrid_layer(x, mem, cos, sin, g_mix[l], w_in[l], g_qa[l], w_qb[l], g_kva[l], w_kvb[l],
                         g_qn_nope[l], g_qn_pe[l], g_kn_nope[l], g_kn_pe[l], conv_qk[l], b_if[l],
                         g_hnorm[l], p_a[l], p_b[l], w_out[l], g_cross[l], g_mem[l], wq_c[l], wk_c[l],
                         wv_c[l], g_cq[l], g_ck[l], wo_c[l], g_ffn[l], w_up[l], conv_ffn[l],
                         b_conv_ffn[l], w_down[l])
    return x


_drawn_inputs = setup_inputs


def setup_inputs(seed=0):
    import zlib

    import numpy as np

    out = dict(_drawn_inputs(seed))
    spreads = {}
    factors = {'g_qa': 8.0,
     'g_kva': 8.0,
     'g_qn_nope': 8.0,
     'g_qn_pe': 8.0,
     'g_kn_nope': 8.0,
     'g_kn_pe': 8.0,
     'g_hnorm': 3.684,
     'g_cross': 8.0,
     'g_mem': 7.056,
     'g_cq': 8.0,
     'g_ck': 8.0,
     'b_conv_ffn': 54.561,
     'g_ffn': 8.0}
    for name, (base, spread) in spreads.items():
        noise = np.random.default_rng([zlib.crc32(name.encode()), seed]).standard_normal(out[name].shape)
        drawn = base * np.exp(spread * noise) if base else spread * noise
        out[name] = __import__('jax').numpy.asarray(drawn.astype(out[name].dtype))
    for name, factor in factors.items():
        out[name] = (out[name] * factor).astype(out[name].dtype)
    return out
```

```python
import numpy as np
from contextlib import ExitStack

import concourse.bass as bass
from concourse import mybir

F32 = mybir.dt.float32
F32R = mybir.dt.float32r
BF16 = mybir.dt.bfloat16
I32 = mybir.dt.int32
ALU = mybir.AluOpType
ACT = mybir.ActivationFunctionType
AX_X = mybir.AxisListType.X

P = 128
D = 2048
T = 256
TT = T // P
KC = D // P
EPS = 1e-6
LORA = 512
LC = LORA // P
MLA_HEADS = 16
PAIRS = MLA_HEADS // 2
NOPE, ROPE = 128, 64
ROPE_BASE = 10000.0
MLA_SCALE = float(NOPE + ROPE) ** -0.5
ML_HEADS, ML_DK, ML_DV = 8, 128, 256
ML_SCALE = float(ML_DK) ** -0.5
CROSS_HEADS = 4
CROSS_SCALE = 128.0 ** -0.5
D_FF = 5632
FC = D_FF // P
CHUNK = 64
BLK = 512
NBLK = D // BLK
KPB = KC // 2

SLOTS = 4
N_NARROW = 2
G_QA = N_NARROW
G_KV = G_QA + KPB
G_MLA = G_KV + KPB
MLA_PER = 2 + 2 + KPB
G_ZO = G_MLA + PAIRS * MLA_PER
G_ML = G_ZO + KPB
G_MERGE = G_ML + NBLK * KPB
G_WOUT = G_MERGE + 4 * NBLK * KPB - KPB
G_CK = G_WOUT + NBLK * KPB
G_CV = G_CK + KPB
G_CQ = G_CV + KPB
G_WO = G_CQ + KPB
G_UP = G_WO + NBLK * 2
UP_ITER = D_FF // BLK
UP_PER = 2 * KPB
G_DOWN = G_UP + UP_ITER * UP_PER
DOWN_PER = 8
DOWN_ITER = FC * 2 // DOWN_PER
G_END = G_DOWN + FC * 2

COLS = {}
_at = 0
for _name, _n in (("g_mix", KC), ("g_mem", KC), ("g_cross", KC), ("g_ffn", KC), ("g_qa", LC), ("g_kva", LC),
                  ("g_hnorm", KC), ("g_qn_nope", 1), ("g_kn_nope", 1), ("g_qn_pe", 1), ("g_kn_pe", 1),
                  ("g_cq", 1), ("g_ck", 1), ("inv_freq", 1), ("b_i", 1), ("b_f", 1),
                  ("conv_qk", 64), ("conv_ffn", 2 * FC * 4)):
    COLS[_name] = _at
    _at += _n
NCOLS = _at


class Pos:

    def __init__(self, base, j=0, per=0):
        self.base, self.j, self.per = base, j, per

    def n(self, c):
        return self.base + c if self.per == 0 else self.per * self.j + (self.base + c)

    def slot(self, c):
        return (self.base + c) % SLOTS

    def landed(self, c):
        uses = (self.base + c) // SLOTS + 1
        return 16 * uses if self.per == 0 else (16 * self.per // SLOTS) * self.j + 16 * uses


def build(nc, x, mem, positions, cols_d, mats_d, stream, out):
    ctx = ExitStack()
    with ctx:
        def sb(name, shape, dt=F32):
            return ctx.enter_context(nc.sbuf_tensor(name, shape, dt))

        made = {}

        def sem(name):
            if name not in made:
                made[name] = ctx.enter_context(nc.semaphore(name))
            return made[name]

        def region(name, nbytes, *plans):
            res = {}
            for plan in plans:
                with ExitStack() as s:
                    for tname, shape, dt in plan:
                        res[tname] = s.enter_context(nc.sbuf_tensor(tname, shape, dt))
            ctx.enter_context(nc.sbuf_tensor(name, [P, nbytes // 4], F32))
            return res

        cols = sb("cols", [P, NCOLS])
        mats = sb("mats", [P, 5 * P])
        ident, rot = mats[:, 0:P], mats[:, P:2 * P]
        mean_nope, mean_pe, tri = mats[:, 2 * P:3 * P], mats[:, 3 * P:4 * P], mats[:, 4 * P:5 * P]
        ones8 = sb("ones8", [8, P])
        q_early = sb("q_early", [1, P], BF16)
        k_late = sb("k_late", [1, P], BF16)
        tiny = sb("tiny", [P, 64])
        a_tok = sb("a_tok", [P, TT, 8])
        e_tok = sb("e_tok", [P, TT, 8])

        w_raw = sb("w_raw", [P, SLOTS, 1024])
        w_hi = sb("w_hi", [P, SLOTS, 1024], F32R)
        w_lo = sb("w_lo", [P, SLOTS, 1024], F32R)

        u = sb("u", [P, KC, 2, T], F32R)
        rb = region("rb_rc", 2 * 32768,
                    [("y_a", [P, KC, 2, T], F32R), ("y_b", [P, KC, 2, T], F32R)],
                    [("rb_pad", [P, 8192], F32), ("qa_t", [P, LC, 2, T], F32R), ("kv_t", [P, LC, 2, T], F32R)],
                    [("mem_t", [P, KC, 2, T], F32R), ("mem_tok", [P, TT, D], F32), ("mem_n", [P, TT, D], F32)],
                    [("rb_pad2", [P, 8192], F32), ("ck", [P, 4, T], F32), ("cv", [P, TT, BLK], F32),
                     ("cq", [P, 4, T], F32), ("c_sq", [P, 4, T], F32),
                     ("c_p", [P, 4, TT, T], F32), ("c_pt", [P, 4, TT, T], F32)],
                    [("h_ff", [P, FC, T], F32)])
        y_a, y_b, qa_t, kv_t, mem_t = rb["y_a"], rb["y_b"], rb["qa_t"], rb["kv_t"], rb["mem_t"]
        mem_tok, mem_n, ck, cv, cq, c_sq, c_p, c_pt, h_ff = (
            rb[n] for n in ("mem_tok", "mem_n", "ck", "cv", "cq", "c_sq", "c_p", "c_pt", "h_ff"))
        DV1 = ML_DV + 1
        zv_b = TT * ML_HEADS * DV1 * 4
        zz = region(
            "zz", 16448 + 16384 + 24 * 1024,
            [("x0_n", [P, TT, D], F32), ("x0_pad", [P, 16], F32), ("x0_tok", [P, TT, D], F32)],
            [("zv_pad", [P, zv_b // 4], F32), ("lat_tok", [P, 2, TT, LORA], F32), ("kpx", [ROPE, 3, T], F32),
             ("zi8", [8, T], F32), ("zf8", [8, T], F32), ("g8a", [8, T], F32), ("g8b", [8, T], F32)],
            [("v_aug", [P, TT, ML_HEADS, DV1], F32), ("qk", [P, 16, T], F32),
             ("cos_t", [P, T], F32), ("sin_t", [P, T], F32), ("kpe", [P, T], F32), ("ncm", [8, T], F32),
             ("gq", [P, 2, T], F32), ("gk", [P, 2, T], F32), ("gp", [P, T], F32),
             ("sq_q", [P, 2, T], F32), ("sq_k", [P, 2, T], F32), ("sq_p", [P, T], F32),
             ("v_pair", [P, TT, 2, P], F32), ("pr", [P, 2, 384], F32), ("prt", [P, 2, 384], F32)],
            [("mpad", [P, zv_b // 4 + 16 * T + 4 * T], F32),
             ("sig", [P, TT, BLK], F32), ("k_st", [P, 2, T], F32), ("m_st", [8, 2, T], F32),
             ("w_ml", [P, 2, 384], F32), ("hn", [P, 2, TT, T], F32), ("junk", [P, T], F32)],
            [("mg_t", [P, KC, 2, T], F32R), ("mg_pad", [P, (zv_b + 16384 + 4096 - 32768) // 4], F32),
             ("mg_sig", [P, TT, BLK], F32), ("sgb", [P, TT, BLK], F32), ("mg_a", [P, TT, BLK], F32),
             ("mg", [P, TT, BLK], F32)],
            [("xn", [P, TT, D], F32), ("yc", [P, 4, 2, T], F32R), ("x_pad", [P, 2048], F32),
             ("x_tok", [P, TT, D], F32)],
            [("ua", [P, 4, T], F32), ("ub", [P, 4, T], F32)],
            [("dpad", [P, 4096], F32), ("h_st", [P, 4, 2, T], F32R)])
        (x0_n, x0_tok, lat_tok, kpx, zi8, zf8, g8a, g8b, v_aug, qk, cos_t, sin_t, kpe, ncm, gq, gk, gp, sq_q, sq_k,
         sq_p, v_pair, pr, prt, sig, k_st, m_st, w_ml, hn, junk, mg_t, sgb, mg_a, mg, xn, yc, x_tok, ua, ub, h_st) = (
            zz[n] for n in ("x0_n", "x0_tok", "lat_tok", "kpx", "zi8", "zf8", "g8a", "g8b", "v_aug", "qk", "cos_t",
                            "sin_t", "kpe", "ncm", "gq", "gk", "gp", "sq_q", "sq_k", "sq_p", "v_pair", "pr", "prt",
                            "sig", "k_st", "m_st", "w_ml", "hn", "junk", "mg_t", "sgb", "mg_a", "mg", "xn", "yc",
                            "x_tok", "ua", "ub", "h_st"))
        ps = ctx.enter_context(nc.psum_tensor("ps", [P, 8, BLK], F32))
        GEMM, ATT = 0, 4

        landed = [sem(f"landed{i}") for i in range(SLOTS)]
        hi_made, lo_made, w_used = sem("hi_made"), sem("lo_made"), sem("w_used")

        def col(name, i=0, rows=slice(0, P)):
            c = COLS[name] + i
            return cols[rows, c:c + 1]

        def dcol(name, i):
            return cols[:, bass.ds(i + COLS[name], 1)] if not isinstance(i, int) else col(name, i)

        block = ctx.enter_context(nc.Block())

        @block.sync
        def _(sp):
            for t in range(TT):
                sp.dma_start(x0_tok[:, t, :], x[t * P:(t + 1) * P, :]).then_inc(sem(f"x_landed{t}"), 16)
            for g in range(SLOTS):
                sp.dma_start(w_raw[:, g, :], stream[g]).then_inc(landed[g], 16)
            turns = G_END // SLOTS - 1
            with sp.Fori(0, turns) as j:
                for g in range(SLOTS):
                    sp.wait_ge(lo_made, SLOTS * j + (g + 1))
                    sp.wait_ge(landed[g], 16)
                    sp.dma_start(w_raw[:, g, :],
                                 stream[bass.ds(SLOTS * j + (SLOTS + g), 1)].rearrange("o p n -> p (o n)")
                                 ).then_inc(landed[g], 16)
            for g in range(G_END - G_END % SLOTS, G_END):
                sp.wait_ge(lo_made, g - SLOTS + 1)
                sp.dma_start(w_raw[:, g % SLOTS, :], stream[g]).then_inc(landed[g % SLOTS], 16)
            for n in range(NBLK):
                for t in range(TT):
                    sp.wait_ge(sem("out_made"), n * TT + t + 1)
                    sp.dma_start(out[t * P:(t + 1) * P, n * BLK:(n + 1) * BLK],
                                 x_tok[:, t, n * BLK:(n + 1) * BLK]).then_inc(sem("stored"), 16)
            sp.wait_ge(sem("stored"), 16 * NBLK * TT)

        @block.gpsimd
        def _(pool):
            pool.dma_start(cols[:], cols_d).then_inc(sem("cols_landed"), 16)
            pool.dma_start(mats[:], mats_d).then_inc(sem("mats_landed"), 16)
            pool.dma_start(gq[:, 0, :].bitcast(I32), positions.partition_broadcast(P)).then_inc(sem("pos_landed"), 16)
            pool.wait_ge(sem("kpe_made"), 1)
            pool.dma_start(kpe[ROPE:2 * ROPE, :], kpe[0:ROPE, :]).then_inc(sem("kpe_copied"), 16)
            pool.wait_ge(w_used, G_WOUT)
            for t in range(TT):
                pool.dma_start(mem_tok[:, t, :], mem[t * P:(t + 1) * P, :]).then_inc(sem(f"mem_landed{t}"), 16)
            pool.wait_ge(sem("mg_lo"), 2 * NBLK)
            for t in range(TT):
                pool.dma_start(x_tok[:, t, :], x[t * P:(t + 1) * P, :]).then_inc(sem(f"x_again{t}"), 16)

        @block.tensor
        def _(pe):
            def by_tokens(pos, c, act, kc0, last_kc, banks):
                s = pos.slot(c)
                pe.wait_ge(lo_made, pos.n(c) + 1)
                for k in range(2):
                    kc = kc0 + k
                    for t in range(TT):
                        a_hi, a_lo = (act[:, kc, half, t * P:(t + 1) * P] for half in (0, 1))
                        b_hi, b_lo = (w[:, s, k * BLK:(k + 1) * BLK] for w in (w_hi, w_lo))
                        o = ps[:, banks + t, :]
                        pe.matmul(o, a_hi, b_hi, start=(kc == 0), stop=False)
                        pe.matmul(o, a_hi, b_lo, start=False, stop=False)
                        mm = pe.matmul(o, a_lo, b_hi, start=False, stop=(kc == last_kc))
                mm.then_inc(w_used, 1)

            def feature_tile(o, s, lo, hi, act, kc, first, last):
                a_hi, a_lo = act[:, kc, 0, :], act[:, kc, 1, :]
                pe.matmul(o, w_hi[:, s, lo:hi], a_hi, start=first, stop=False, skip_group_check=True)
                pe.matmul(o, w_hi[:, s, lo:hi], a_lo, start=False, stop=False, skip_group_check=True)
                return pe.matmul(o, w_lo[:, s, lo:hi], a_hi, start=False, stop=last, skip_group_check=True)

            def by_features(pos, c, act, kc0, banks):
                s = pos.slot(c)
                pe.wait_ge(lo_made, pos.n(c) + 1)
                for k in range(2):
                    kc = kc0 + k
                    for m in range(4):
                        o = ps[:, banks + m // 2, (m % 2) * T:(m % 2 + 1) * T]
                        mm = feature_tile(o, s, k * BLK + m * P, k * BLK + (m + 1) * P, act, kc,
                                          kc == 0 and m % 2 == 0, kc == KC - 1)
                mm.then_inc(w_used, 1)

            def transposed(n, src):
                pe.wait_ge(sem("norm_xn0"), n + 1)
                pe.wait_ge(sem("norm_xn1"), n + 1)
                for i in range(KC // 2):
                    if i >= 4:
                        pe.wait_ge(sem("norm_lo"), KC * n + 2 * (i - 3))
                    for k in range(2):
                        for t in range(TT):
                            kc = 2 * i + k
                            mm = pe.transpose(ps[:, ATT + i % 4, k * T + t * P:k * T + (t + 1) * P],
                                              src[:, t, kc * P:(kc + 1) * P], ident)
                    mm.then_inc(sem("norm_T"), 1)

            pe.wait_ge(sem("mats_landed"), 16)
            transposed(0, x0_n)
            pe.wait_ge(sem("norm_lo"), KC * 1)

            pos = Pos(0)
            for c in range(N_NARROW):
                pe.wait_ge(lo_made, c + 1)
                for k in range(8):
                    kc = 8 * c + k
                    mm = feature_tile(ps[:, ATT, 0:T], c, k * P, (k + 1) * P, u, kc, kc == 0, kc == KC - 1)
                mm.then_inc(w_used, 1)
            for c in range(KPB):
                by_tokens(pos, G_QA + c, u, 2 * c, KC - 1, GEMM)
                if c == 2:
                    pe.wait_ge(sem("kpx_made"), 2)
                    pe.matmul(ps[0:ROPE, ATT + 1, 0:T], mean_pe[0:ROPE, 0:ROPE], kpx[:, 0, :], start=True, stop=True)
                    pe.wait_ge(sem("kpg_made"), 1)
                    pe.matmul(ps[0:ROPE, ATT + 1, T:2 * T], rot[0:ROPE, 0:ROPE], kpx[:, 1, :], start=True, stop=True,
                              skip_group_check=True).then_inc(sem("kp_rot"), 1)

            def latent_T(i):
                pe.wait_ge(sem("lat_n"), TT * (i + 1))
                for b in range(2):
                    if i == 1 and b == 0:
                        pe.wait_ge(sem("lat_lo"), LC)
                    for k in range(2):
                        for t in range(TT):
                            kc = 2 * b + k
                            mm = pe.transpose(ps[:, ATT + 2 + b, k * T + t * P:k * T + (t + 1) * P],
                                              lat_tok[:, i, t, kc * P:(kc + 1) * P], ident)
                    mm.then_inc(sem("lat_T"), 1)

            for c in range(KPB):
                by_tokens(pos, G_KV + c, u, 2 * c, KC - 1, GEMM + 2)
                if c == 4:
                    latent_T(0)
                if c == 6:
                    pe.wait_ge(sem("gates_made"), 1)
                    for t in range(TT):
                        pe.transpose(ps[:, ATT, t * 8:t * 8 + 8], g8a[:, t * P:(t + 1) * P], ident[0:8, 0:8])
                    for t in range(TT):
                        mm = pe.transpose(ps[:, ATT, 16 + t * 8:24 + t * 8], g8b[:, t * P:(t + 1) * P],
                                          ident[0:8, 0:8])
                    mm.then_inc(sem("gates_T"), 1)
            latent_T(1)
            pe.wait_ge(sem("lat_lo"), 2 * LC)

            def mla_pass(pos, it, filler):
                def fill(i):
                    if filler == "qk":
                        by_features(pos, 4 + i, u, 2 * i, GEMM)
                    else:
                        by_tokens(pos, 4 + i, u, 2 * i, KC - 1, GEMM)

                A0, A1, A2, A3 = ATT, ATT + 1, ATT + 2, ATT + 3
                pe.wait_ge(sem("ya_lo"), it + 1)
                for c in range(2):
                    s = pos.slot(c)
                    pe.wait_ge(lo_made, pos.n(c) + 1)
                    for k in range(2):
                        kc = 2 * c + k
                        for h in range(2):
                            feature_tile(ps[:, A0, h * T:(h + 1) * T], s, k * BLK + h * P, k * BLK + (h + 1) * P,
                                         qa_t, kc, kc == 0 and h == 0, kc == LC - 1)
                        mm = feature_tile(ps[:, A3, 0:T], s, k * BLK + 2 * P, k * BLK + 3 * P, qa_t, kc, kc == 0,
                                          kc == LC - 1)
                    mm.then_inc(w_used, 1)
                for c in range(2, 4):
                    s = pos.slot(c)
                    pe.wait_ge(lo_made, pos.n(c) + 1)
                    for k in range(2):
                        kc = 2 * (c - 2) + k
                        for h in range(2):
                            feature_tile(ps[:, A1, h * T:(h + 1) * T], s, k * BLK + h * P, k * BLK + (h + 1) * P,
                                         kv_t, kc, kc == 0 and h == 0, kc == LC - 1)
                        for t in range(TT):
                            o = ps[:, A2, t * T:(t + 1) * T]
                            a_hi, a_lo = (kv_t[:, kc, half, t * P:(t + 1) * P] for half in (0, 1))
                            b_hi, b_lo = (w[:, s, k * BLK + T:(k + 1) * BLK] for w in (w_hi, w_lo))
                            pe.matmul(o, a_hi, b_hi, start=(kc == 0 and t == 0), stop=False, skip_group_check=True)
                            pe.matmul(o, a_hi, b_lo, start=False, stop=False, skip_group_check=True)
                            mm = pe.matmul(o, a_lo, b_hi, start=False, stop=(kc == LC - 1), skip_group_check=True)
                    mm.then_inc(w_used, 1)
                fill(0)
                fill(1)
                pe.wait_ge(sem("gq_made"), it + 1)
                pe.matmul(ps[:, A0, :], mean_nope, sq_q[:].rearrange("p h t -> p (h t)"), start=True, stop=True
                          ).then_inc(sem("ms_q"), 1)
                pe.wait_ge(sem("gp_made"), it + 1)
                pe.matmul(ps[:, A3, 0:T], mean_pe, sq_p[:], start=True, stop=True)
                pe.matmul(ps[:, A3, T:2 * T], rot, gp[:], start=True, stop=True, skip_group_check=True
                          ).then_inc(sem("ms_p"), 1)
                pe.wait_ge(sem("gk_made"), it + 1)
                pe.matmul(ps[:, A1, :], mean_nope, sq_k[:].rearrange("p h t -> p (h t)"), start=True, stop=True
                          ).then_inc(sem("ms_k"), 1)
                fill(2)
                fill(3)
                pe.wait_ge(sem("qk_ready"), it + 1)
                pe.wait_ge(sem("kpe_copied"), 16)
                for h in range(2):
                    rows = slice(h * ROPE, (h + 1) * ROPE)
                    for t in range(TT):
                        o = ps[:, A0 + h, t * P:t * P + (t + 1) * P]
                        q = slice(t * P, (t + 1) * P)
                        keys = slice(0, (t + 1) * P)
                        pe.matmul(o, gq[:, h, q], gk[:, h, keys], start=(t == 0), stop=False, skip_group_check=True)
                        pe.matmul(o, gp[rows, q], kpe[rows, keys], start=False, stop=False, skip_group_check=True)
                        diag = ps[:, A0 + h, 2 * t * P:(2 * t + 1) * P]
                        mm = pe.matmul(diag, q_early[:], k_late[:], start=False, stop=True, skip_group_check=True)
                    mm.then_inc(sem("scored"), 1)
                fill(4)
                fill(5)
                pe.wait_ge(sem("p_ready"), it + 1)
                for h in range(2):
                    for src, dst in ((0, 0), (1, 1), (2, 2)):
                        mm = pe.transpose(ps[:, A0 + h, dst * P:(dst + 1) * P], pr[:, h, src * P:(src + 1) * P], ident)
                    mm.then_inc(sem("pT"), 1)
                fill(6)
                fill(7)
                pe.wait_ge(sem("pt_ready"), 2 * it + 2)
                for h in range(2):
                    o = ps[:, A2, h * T:(h + 1) * T]
                    pe.matmul(o, v_pair[:, 0, h, :], prt[:, h, 0:T], start=(h == 0), stop=False,
                              skip_group_check=True)
                    mm = pe.matmul(ps[:, A2, h * T + P:(h + 1) * T], v_pair[:, 1, h, :], prt[:, h, T:T + P],
                                   start=False, stop=True, skip_group_check=True)
                mm.then_inc(sem("attended"), 1)

            with pe.Fori(0, 4) as j:
                mla_pass(Pos(G_MLA, j, MLA_PER), j, "qk")
            with pe.Fori(0, 4) as j:
                mla_pass(Pos(G_MLA + 4 * MLA_PER, j, MLA_PER), j + 4, "v")

            pe.wait_ge(sem("zv_read"), TT * 4)
            for c in range(KPB):
                by_tokens(Pos(G_ZO), c, u, 2 * c, KC - 1, GEMM)

            with pe.Fori(0, NBLK) as j:
                pos = Pos(G_ML, j, KPB)
                pe.wait_ge(sem("sig_made"), TT * j + TT)
                by_tokens(pos, 0, u, 0, KC - 1, GEMM)
                by_tokens(pos, 1, u, 2, KC - 1, GEMM)
                pe.wait_ge(sem("k_staged"), j + 1)
                pe.wait_ge(sem("m_staged"), 2 * j + 2)
                for i in range(2):
                    q_all = qk[:, bass.ds(2 * j + i, 1), :]
                    q_late = qk[:, bass.ds(2 * j + i, 1), P:T]
                    pe.matmul(ps[:, ATT + i, 0:T], k_st[:, i, 0:P], q_all, start=True, stop=True,
                              skip_group_check=True)
                    mm = pe.matmul(ps[:, ATT + i, T:T + P], k_st[:, i, P:T], q_late, start=True, stop=True,
                                   skip_group_check=True)
                mm = pe.matmul(ps[:, ATT + 2, :], ones8[:], m_st[:].rearrange("p h t -> p (h t)"), start=True,
                               stop=True).then_inc(sem("ml_scored"), 1)
                for c in (2, 3, 4):
                    by_tokens(pos, c, u, 2 * c, KC - 1, GEMM)
                pe.wait_ge(sem("ml_p"), 2 * j + 2)
                for i in range(2):
                    v0, v1 = (v_aug[:, t, bass.ds(2 * j + i, 1), :] for t in range(TT))
                    pe.matmul(ps[:, ATT + 2 * i, 0:DV1], w_ml[:, i, 0:P], v0, start=True, stop=True)
                    pe.matmul(ps[:, ATT + 2 * i + 1, 0:DV1], w_ml[:, i, P:T], v0, start=True, stop=False)
                    mm = pe.matmul(ps[:, ATT + 2 * i + 1, 0:DV1], w_ml[:, i, T:T + P], v1, start=False, stop=True)
                mm.then_inc(sem("ml_num"), 1)
                for c in (5, 6, 7):
                    by_tokens(pos, c, u, 2 * c, KC - 1, GEMM)
                pe.wait_ge(sem("yb_tok"), 4 * j + 4)
                for i in range(2):
                    for half in range(2):
                        for t in range(TT):
                            mm = pe.transpose(ps[:, ATT + i, half * T + t * P:half * T + (t + 1) * P],
                                              hn[:, i, t, half * P:(half + 1) * P], ident)
                    mm.then_inc(sem("yb_T"), 1)

            def merge_pass(pos, it, last):
                for c in range(KPB):
                    by_tokens(pos, c, y_a, 2 * c, KC - 1, GEMM)
                for c in range(KPB):
                    by_tokens(pos, KPB + c, u, 2 * c, KC - 1, GEMM + 2)
                for c in range(KPB):
                    by_tokens(pos, 2 * KPB + c, y_b, 2 * c, KC - 1, ATT)
                if not last:
                    pe.wait_ge(sem("sig_made"), TT * (NBLK + 1) + TT * it)
                    for c in range(4):
                        by_tokens(pos, 3 * KPB + c, u, 2 * c, KC - 1, ATT + 2)
                pe.wait_ge(sem("mg_made"), it + 1)
                for b in range(2):
                    for k in range(2):
                        for t in range(TT):
                            kc = 2 * b + k
                            mm = pe.transpose(ps[:, GEMM + b, k * T + t * P:k * T + (t + 1) * P],
                                              mg[:, t, kc * P:(kc + 1) * P], ident)
                    mm.then_inc(sem("mg_T"), 1)
                if not last:
                    for c in range(4, KPB):
                        by_tokens(pos, 3 * KPB + c, u, 2 * c, KC - 1, ATT + 2)

            pe.wait_ge(sem("yb_lo"), 4 * NBLK)
            with pe.Fori(0, NBLK - 1) as j:
                merge_pass(Pos(G_MERGE, j, 4 * KPB), j, False)
            pe.wait_ge(sem("mg_lo"), 2 * (NBLK - 1))
            merge_pass(Pos(G_MERGE + 4 * KPB * (NBLK - 1)), NBLK - 1, True)

            pe.wait_ge(sem("mg_lo"), 2 * NBLK)
            with pe.Fori(0, 2) as j:
                for n in range(2):
                    for c in range(KPB):
                        by_tokens(Pos(G_WOUT, j, 2 * KPB), n * KPB + c, mg_t, 2 * c, KC - 1, GEMM + 2 * n)

            transposed(1, mem_n)
            pe.wait_ge(sem("norm_lo"), KC * 2)
            pe.wait_ge(sem("x1_made"), 2 * TT * 2)
            for c in range(KPB):
                by_features(Pos(G_CK), c, mem_t, 2 * c, GEMM)
            for c in range(KPB):
                by_tokens(Pos(G_CV), c, mem_t, 2 * c, KC - 1, GEMM + 2)

            def mean_squares(n):
                pe.wait_ge(sem("c_g"), n + 1)
                for b in range(2):
                    mm = pe.matmul(ps[:, ATT + b, :], mean_nope, c_sq[:, 2 * b:2 * b + 2, :], start=True, stop=True)
                mm.then_inc(sem("c_ms"), 1)

            transposed(2, xn)
            pe.wait_ge(sem("norm_lo"), KC * 3)
            mean_squares(0)
            for c in range(KPB):
                by_features(Pos(G_CQ), c, u, 2 * c, GEMM)
            mean_squares(1)
            pe.wait_ge(sem("c_ready"), 2)
            for h in range(CROSS_HEADS):
                for t in range(TT):
                    mm = pe.matmul(ps[:, ATT + h, t * T:(t + 1) * T], cq[:, h, t * P:(t + 1) * P], ck[:, h, :],
                                   start=True, stop=True, skip_group_check=True)
                mm.then_inc(sem("c_scored"), 1)
            for h in range(CROSS_HEADS):
                pe.wait_ge(sem("c_p_ready"), h + 1)
                for s in range(TT):
                    for t in range(TT):
                        mm = pe.transpose(ps[:, ATT + h, s * T + t * P:s * T + (t + 1) * P],
                                          c_p[:, h, t, s * P:(s + 1) * P], ident)
                mm.then_inc(sem("c_pT"), 1)
            for h in range(CROSS_HEADS):
                pe.wait_ge(sem("c_pt_ready"), h + 1)
                o = ps[:, GEMM + h // 2, (h % 2) * T:(h % 2 + 1) * T]
                for s in range(TT):
                    mm = pe.matmul(o, cv[:, s, h * P:(h + 1) * P], c_pt[:, h, s, :], start=(s == 0), stop=(s == 1),
                                   skip_group_check=True)
                if h % 2:
                    mm.then_inc(sem("c_att"), 1)
            pe.wait_ge(sem("yc_lo"), 2)
            for n in range(NBLK):
                for c in range(2):
                    by_tokens(Pos(G_WO), 2 * n + c, yc, 2 * c, 3, 2 * n)

            transposed(3, xn)
            pe.wait_ge(sem("norm_lo"), KC * 4)
            with pe.Fori(0, UP_ITER) as j:
                pos = Pos(G_UP, j, UP_PER)
                for c in range(KPB):
                    by_features(pos, c, u, 2 * c, GEMM)
                for c in range(KPB):
                    by_features(pos, KPB + c, u, 2 * c, GEMM + 2)

            def down_pass(pos, it, first, last):
                for c in range(DOWN_PER):
                    s, kc, half = pos.slot(c), c // 2, c % 2
                    pe.wait_ge(lo_made, pos.n(c) + 1)
                    if half == 0:
                        pe.wait_ge(sem("hst_lo"), 4 * it + (kc + 1))
                    for t in range(TT):
                        a_hi, a_lo = (h_st[:, kc, hl, t * P:(t + 1) * P] for hl in (0, 1))
                        for n in range(2):
                            o = ps[:, t * 4 + half * 2 + n, :]
                            b_hi, b_lo = (w[:, s, n * BLK:(n + 1) * BLK] for w in (w_hi, w_lo))
                            pe.matmul(o, a_hi, b_hi, start=(first and kc == 0), stop=False, skip_group_check=True)
                            pe.matmul(o, a_hi, b_lo, start=False, stop=False, skip_group_check=True)
                            mm = pe.matmul(o, a_lo, b_hi, start=False, stop=(last and kc == 3),
                                           skip_group_check=True)
                    mm.then_inc(w_used, 1)

            pe.wait_ge(sem("fb_taps"), 8 * UP_ITER)
            down_pass(Pos(G_DOWN), 0, True, False)
            with pe.Fori(0, DOWN_ITER - 2) as j:
                down_pass(Pos(G_DOWN + DOWN_PER, j, DOWN_PER), j + 1, False, False)
            down_pass(Pos(G_DOWN + DOWN_PER * (DOWN_ITER - 1)), DOWN_ITER - 1, False, True)

        @block.scalar
        def _(act):
            def split(pos, c):
                if pos.per == 0 and pos.base + c + SLOTS >= G_END:
                    return
                s = pos.slot(c)
                act.wait_ge(landed[s], pos.landed(c + SLOTS))
                act.wait_ge(w_used, pos.n(c) + 1)
                act.activation(w_hi[:, s, :], w_raw[:, s, :], ACT.Copy).then_inc(hi_made, 1)

            def norm_begin(n, src, scratch, ready):
                for t in range(TT):
                    act.wait_ge(*ready[t])
                    act.activation(scratch[:, t, :], src[:, t, :], ACT.Square, accum_out=tiny[:, t:t + 1]
                                   ).then_inc(sem("norm_ss"), 1)
                act.wait_ge(sem("norm_mv"), n + 1)
                act.activation(tiny[:, 4:6], tiny[:, 2:4], ACT.Sqrt).then_inc(sem("norm_rt"), 1)
                act.wait_ge(sem("norm_r"), n + 1)
                act.wait_ge(sem("norm_ss"), TT * (n + 1))
                act.activation(scratch[:, 1, :], src[:, 1, :], ACT.Copy, scale=tiny[:, 7:8]
                               ).then_inc(sem("norm_xn1"), 1)

            def norm_end(n, dst, gain):
                for i in range(KC // 2):
                    act.wait_ge(sem("norm_T"), KC // 2 * n + i + 1)
                    for k in range(2):
                        kc = 2 * i + k
                        act.activation(dst[:, kc, 0, :], ps[:, ATT + i % 4, k * T:(k + 1) * T], ACT.Copy,
                                       scale=col(gain, kc)).then_inc(sem("norm_hi"), 1)

            for g in range(SLOTS):
                act.wait_ge(landed[g], 16)
                act.activation(w_hi[:, g, :], w_raw[:, g, :], ACT.Copy).then_inc(hi_made, 1)
                if g == 0:
                    norm_begin(0, x0_tok, x0_n, [(sem("x_landed0"), 16), (sem("x_landed1"), 16)])
            act.wait_ge(sem("cols_landed"), 16)
            norm_end(0, u, "g_mix")
            act.wait_ge(sem("angles"), 1)
            act.activation(sin_t[:], gk[:, 0, :], ACT.Sin).then_inc(sem("tables"), 1)
            act.activation(cos_t[:], gk[:, 1, :], ACT.Sin).then_inc(sem("tables"), 1)
            pos = Pos(0)
            for c in range(N_NARROW):
                split(pos, c)
            act.activation(kpx[:, 2, :], ps[0:ROPE, ATT, 0:T], ACT.Copy).then_inc(sem("kpx_made"), 1)
            act.activation(kpx[:, 0, :], ps[0:ROPE, ATT, 0:T], ACT.Square).then_inc(sem("kpx_made"), 1)
            act.activation(zi8[:], ps[64:72, ATT, 0:T], ACT.Copy).then_inc(sem("z8"), 1)
            act.activation(zf8[:], ps[96:104, ATT, 0:T], ACT.Copy).then_inc(sem("z8"), 1)
            for c in range(KPB):
                split(pos, G_QA + c)
                if c == 0:
                    act.wait_ge(sem("f_made"), 1)
                    act.activation(g8a[:], zf8[:], ACT.Abs).then_inc(sem("ls_act"), 1)
                    act.wait_ge(sem("ls_act"), 1)
                    act.activation(g8b[:], g8a[:], ACT.Exp, scale=-1.0).then_inc(sem("ls_act"), 1)
                if c == 1:
                    act.wait_ge(sem("e_plus"), 1)
                    act.activation(g8a[:], g8b[:], ACT.Ln).then_inc(sem("ls_act"), 1)
                if c == 3:
                    act.wait_ge(sem("kp_rot"), 1)
                    act.wait_ge(sem("kp_mv"), 1)
                    act.activation(kpx[:, 0, :], kpx[:, 0, :], ACT.Sqrt).then_inc(sem("kp_rt"), 1)
                if c == 5:
                    act.wait_ge(sem("m_neg"), 1)
                    act.activation(g8b[:], g8b[:], ACT.Exp, scale=-1.0).then_inc(sem("gates_made"), 1)

            def latent(i, bank):
                for t in range(TT):
                    act.activation(lat_tok[:, i, t, :], ps[:, bank + t, :], ACT.Square,
                                   accum_out=tiny[:, 8 + 2 * i + t:9 + 2 * i + t]).then_inc(sem("lat_ss"), 1)
                act.wait_ge(sem("lat_mv"), i + 1)
                act.activation(tiny[:, 16 + 2 * i:18 + 2 * i], tiny[:, 12 + 2 * i:14 + 2 * i], ACT.Sqrt
                               ).then_inc(sem("lat_rt"), 1)
                act.wait_ge(sem("lat_r"), i + 1)
                act.wait_ge(sem("lat_ss"), TT * (i + 1))
                for t in range(TT):
                    act.activation(lat_tok[:, i, t, :], ps[:, bank + t, :], ACT.Copy,
                                   scale=tiny[:, 20 + 2 * i + t:21 + 2 * i + t]).then_inc(sem("lat_n"), 1)

            def latent_hi(i, dst, gain):
                for b in range(2):
                    act.wait_ge(sem("lat_T"), 2 * i + b + 1)
                    for k in range(2):
                        kc = 2 * b + k
                        act.activation(dst[:, kc, 0, :], ps[:, ATT + 2 + b, k * T:(k + 1) * T], ACT.Copy,
                                       scale=col(gain, kc)).then_inc(sem("lat_hi"), 1)

            latent(0, GEMM)
            for c in range(KPB):
                split(pos, G_KV + c)
                if c == 5:
                    latent_hi(0, qa_t, "g_qa")
                if c == 7:
                    act.wait_ge(sem("gates_T"), 1)
                    act.activation(a_tok[:].rearrange("p t h -> p (t h)"), ps[:, ATT, 0:16], ACT.Copy
                                   ).then_inc(sem("gates_tok"), 1)
                    act.activation(e_tok[:].rearrange("p t h -> p (t h)"), ps[:, ATT, 16:32], ACT.Copy
                                   ).then_inc(sem("gates_tok"), 1)
            latent(1, GEMM + 2)
            latent_hi(1, kv_t, "g_kva")

            def mla_pass(pos, it, filler):
                split(pos, 0)
                split(pos, 1)
                act.activation(sq_q[:].rearrange("p h t -> p (h t)"), ps[:, ATT, :], ACT.Square
                               ).then_inc(sem("sqq_made"), 1)
                act.activation(sq_p[:], ps[:, ATT + 3, 0:T], ACT.Square).then_inc(sem("sqp_made"), 1)
                split(pos, 2)
                split(pos, 3)
                act.activation(sq_k[:].rearrange("p h t -> p (h t)"), ps[:, ATT + 1, :], ACT.Square
                               ).then_inc(sem("sqk_made"), 1)
                act.activation(v_pair[:].rearrange("p t h d -> p (t h d)"), ps[:, ATT + 2, :], ACT.Copy
                               ).then_inc(sem("v_made"), 1)
                split(pos, 4)
                split(pos, 5)
                act.wait_ge(sem("mv_q"), it + 1)
                act.activation(sq_q[:], sq_q[:], ACT.Sqrt).then_inc(sem("rt_q"), 1)
                act.wait_ge(sem("mv_p"), it + 1)
                act.activation(sq_p[:], sq_p[:], ACT.Sqrt).then_inc(sem("rt_p"), 1)
                act.wait_ge(sem("mv_k"), it + 1)
                act.activation(sq_k[:], sq_k[:], ACT.Sqrt).then_inc(sem("rt_k"), 1)
                split(pos, 6)
                split(pos, 7)
                act.wait_ge(sem("neg_max"), it + 1)
                for h in range(2):
                    for t in range(TT):
                        n = 2 * h + t
                        act.activation(pr[:, h, t * P:t * P + (t + 1) * P],
                                       ps[:, ATT + h, t * P:t * P + (t + 1) * P], ACT.Exp,
                                       bias=tiny[:, 28 + n:29 + n], scale=MLA_SCALE,
                                       accum_out=tiny[:, 32 + n:33 + n]).then_inc(sem("p_exp"), 1)
                split(pos, 8)
                split(pos, 9)
                act.wait_ge(sem("pT"), 2 * it + 2)
                act.activation(prt[:, 1, :], ps[:, ATT + 1, 0:384], ACT.Copy).then_inc(sem("pt_1"), 1)
                split(pos, 10)
                split(pos, 11)
                if filler == "qk":
                    for m in range(4):
                        act.activation(qk[:, bass.ds(4 * it + m, 1), :],
                                       ps[:, GEMM + m // 2, (m % 2) * T:(m % 2 + 1) * T], ACT.Copy,
                                       scale=dcol("conv_qk", 16 * it + (4 * m + 3))).then_inc(sem("cv_first"), 1)
                else:
                    for t in range(TT):
                        act.activation(v_aug[:, t, bass.ds(2 * (it - 4), 2), 0:ML_DV],
                                       ps[:, GEMM + t, :].rearrange("p (h d) -> p h d", h=2), ACT.Copy
                                       ).then_inc(sem("zv_read"), 1)
                if filler == "qk":
                    act.wait_ge(sem("cv_taps"), 12 * it + 12)
                act.wait_ge(sem("attended"), it + 1)
                act.activation(y_a[:, bass.ds(2 * it, 2), 0, :],
                               ps[:, ATT + 2, :].rearrange("p (h t) -> p h t", h=2), ACT.Copy
                               ).then_inc(sem("ya_hi"), 1)
                if filler == "qk":
                    act.activation(qk[:, bass.ds(4 * it, 4), :], qk[:, bass.ds(4 * it, 4), :], ACT.Silu
                                   ).then_inc(sem("cv_made"), 1)

            with act.Fori(0, 4) as j:
                mla_pass(Pos(G_MLA, j, MLA_PER), j, "qk")
            with act.Fori(0, 4) as j:
                mla_pass(Pos(G_MLA + 4 * MLA_PER, j, MLA_PER), j + 4, "v")

            def sigmoid_block(bank):
                for t in range(TT):
                    act.activation(sig[:, t, :], ps[:, bank + t, :], ACT.Sigmoid).then_inc(sem("sig_made"), 1)

            for c in range(KPB):
                split(Pos(G_ZO), c)
            act.wait_ge(sem("attended"), PAIRS)
            act.wait_ge(sem("ya_lo"), PAIRS + 1)
            sigmoid_block(GEMM)

            with act.Fori(0, NBLK) as j:
                pos = Pos(G_ML, j, KPB)
                act.wait_ge(sem("cv_made"), 4)
                act.activation(k_st[:], qk[:, bass.ds(2 * j + ML_HEADS, 2), :], ACT.Copy).then_inc(sem("k_staged"), 1)
                for c in range(4):
                    split(pos, c)
                act.wait_ge(sem("ml_arg"), 4 * j + 4)
                for i in range(2):
                    act.activation(w_ml[:, i, :], w_ml[:, i, :], ACT.Exp).then_inc(sem("ml_w"), 1)
                split(pos, 4)
                split(pos, 5)
                act.wait_ge(sem("ml_hn"), 4 * j + 4)
                for i in range(2):
                    for t in range(TT):
                        n = 2 * i + t
                        if n:
                            act.wait_ge(sem("ml_ss"), 4 * j + n)
                        act.activation(junk[:], hn[:, i, t, :], ACT.Square, accum_out=tiny[:, 44 + n:45 + n]
                                       ).then_inc(sem("ml_ss"), 1)
                act.wait_ge(sem("ml_mv"), j + 1)
                act.activation(tiny[:, 48:52], tiny[:, 48:52], ACT.Sqrt).then_inc(sem("ml_rt"), 1)
                split(pos, 6)
                split(pos, 7)
                act.wait_ge(sem("yb_tok"), 4 * j + 4)
                sigmoid_block(GEMM)
                for i in range(2):
                    act.wait_ge(sem("yb_T"), 2 * j + (i + 1))
                    for half in range(2):
                        n = 2 * i + half
                        act.activation(y_b[:, bass.ds(4 * j + n, 1), 0, :],
                                       ps[:, ATT + i, half * T:(half + 1) * T], ACT.Copy,
                                       scale=dcol("g_hnorm", 4 * j + n)).then_inc(sem("yb_hi"), 1)

            def merge_pass(pos, it, last):
                for c in range(2 * KPB):
                    split(pos, c)
                for t in range(TT):
                    act.activation(sgb[:, t, :], ps[:, GEMM + 2 + t, :], ACT.Sigmoid).then_inc(sem("sgb_made"), 1)
                for c in range(2 * KPB, 3 * KPB):
                    split(pos, c)
                if not last:
                    for c in range(3 * KPB, 3 * KPB + 4):
                        split(pos, c)
                for b in range(2):
                    act.wait_ge(sem("mg_T"), 2 * it + (b + 1))
                    act.activation(mg_t[:, bass.ds(4 * it + 2 * b, 2), 0, :],
                                   ps[:, GEMM + b, :].rearrange("p (k t) -> p k t", k=2), ACT.Copy
                                   ).then_inc(sem("mg_hi"), 1)
                if not last:
                    for c in range(3 * KPB + 4, 4 * KPB):
                        split(pos, c)
                    sigmoid_block(ATT + 2)

            with act.Fori(0, NBLK - 1) as j:
                merge_pass(Pos(G_MERGE, j, 4 * KPB), j, False)
            merge_pass(Pos(G_MERGE + 4 * KPB * (NBLK - 1)), NBLK - 1, True)

            for c in range(KPB):
                split(Pos(G_WOUT), c)
            norm_begin(1, mem_tok, mem_n, [(sem("mem_landed0"), 16), (sem("mem_landed1"), 16)])
            with act.Fori(0, NBLK - 1) as j:
                for c in range(KPB):
                    split(Pos(G_WOUT + KPB, j, KPB), c)
            norm_end(1, mem_t, "g_mem")

            norm_begin(2, x_tok, xn, [(sem("x1_made"), NBLK * TT)] * 2)
            for c in range(KPB):
                split(Pos(G_CK), c)

            def c_squares(n):
                for b in range(2):
                    act.activation(c_sq[:, 2 * b:2 * b + 2, :],
                                   ps[:, GEMM + b, :].rearrange("p (h t) -> p h t", h=2), ACT.Square
                                   ).then_inc(sem("c_sqd"), 1)

            def c_root(n):
                act.wait_ge(sem("c_mv"), 2 * n + 2)
                act.activation(c_sq[:], c_sq[:], ACT.Sqrt).then_inc(sem("c_rt"), 1)

            c_squares(0)
            for c in range(KPB):
                split(Pos(G_CV), c)
            for t in range(TT):
                act.activation(cv[:, t, :], ps[:, GEMM + 2 + t, :], ACT.Copy).then_inc(sem("cv_v"), 1)
            norm_end(2, u, "g_cross")
            c_root(0)
            for c in range(KPB):
                split(Pos(G_CQ), c)
            act.wait_ge(sem("c_ready"), 1)
            c_squares(1)
            c_root(1)
            for h in range(CROSS_HEADS):
                act.wait_ge(sem("c_nmax"), h + 1)
                for t in range(TT):
                    n = 2 * h + t
                    act.activation(c_p[:, h, t, :], ps[:, ATT + h, t * T:(t + 1) * T], ACT.Exp,
                                   bias=tiny[:, 8 + n:9 + n], scale=CROSS_SCALE, accum_out=tiny[:, 16 + n:17 + n]
                                   ).then_inc(sem("c_exp"), 1)
            for h in range(0, CROSS_HEADS):
                act.wait_ge(sem("c_pT"), h + 1)
                act.activation(c_pt[:, h, :, :], ps[:, ATT + h, :].rearrange("p (s t) -> p s t", s=TT), ACT.Copy
                               ).then_inc(sem("c_pt_ready"), 1)
            for b in range(2):
                act.wait_ge(sem("c_att"), b + 1)
                act.activation(yc[:, 2 * b:2 * b + 2, 0, :], ps[:, GEMM + b, :].rearrange("p (h t) -> p h t", h=2),
                               ACT.Copy).then_inc(sem("yc_hi"), 1)
            for c in range(2 * NBLK):
                split(Pos(G_WO), c)
            norm_begin(3, x_tok, xn, [(sem("x2_made"), NBLK * TT)] * 2)
            norm_end(3, u, "g_ffn")

            with act.Fori(0, UP_ITER) as j:
                pos = Pos(G_UP, j, UP_PER)
                for half, dst, pre in ((0, ua, "fa"), (1, ub, "fb")):
                    for c in range(KPB):
                        split(pos, half * KPB + c)
                    for m in range(4):
                        at = 16 * j + (half * FC * 4 + 4 * m)
                        act.activation(dst[:, m, :], ps[:, GEMM + 2 * half + m // 2, (m % 2) * T:(m % 2 + 1) * T],
                                       ACT.Identity, scale=dcol("conv_ffn", at + 2), bias=dcol("conv_ffn", at + 3)
                                       ).then_inc(sem(pre + "_first"), 1)
                    if half == 0:
                        act.wait_ge(sem("fa_taps"), 8 * j + 8)
                        act.activation(ua[:], ua[:], ACT.Silu).then_inc(sem("fa_silu"), 1)

            def stage(it, kc):
                act.activation(h_st[:, kc:kc + 1, 0, :], h_ff[:, bass.ds(4 * it + kc, 1), :]
                               if not isinstance(it, int) else h_ff[:, 4 * it + kc:4 * it + kc + 1, :], ACT.Copy
                               ).then_inc(sem("hst_hi"), 1)

            act.wait_ge(sem("h_made"), UP_ITER)
            for kc in range(4):
                stage(0, kc)

            def down_pass(pos, it, last):
                for c in range(DOWN_PER):
                    split(pos, c)
                    if c % 2 and not last:
                        act.wait_ge(sem("hst_lo"), 4 * it + (c // 2 + 1))
                        act.wait_ge(w_used, pos.n(c) + 1)
                        stage(it + 1, c // 2)

            with act.Fori(0, DOWN_ITER - 1) as j:
                down_pass(Pos(G_DOWN, j, DOWN_PER), j, False)
            down_pass(Pos(G_DOWN + DOWN_PER * (DOWN_ITER - 1)), DOWN_ITER - 1, True)

        @block.vector
        def _(dve):
            TTo, TS, STT = dve.tensor_tensor, dve.tensor_scalar, dve.scalar_tensor_tensor

            def split(pos, c):
                if pos.per == 0 and pos.base + c + SLOTS >= G_END:
                    return
                s = pos.slot(c)
                dve.wait_ge(hi_made, pos.n(c) + SLOTS + 1)
                TTo(w_lo[:, s, :], w_raw[:, s, :], w_hi[:, s, :].bitcast(F32), ALU.subtract).then_inc(lo_made, 1)

            def norm_begin(n, src, scratch):
                dve.wait_ge(sem("norm_ss"), TT * (n + 1))
                TS(tiny[:, 2:4], tiny[:, 0:2], 1.0 / D, EPS, ALU.mult, ALU.add).then_inc(sem("norm_mv"), 1)
                dve.wait_ge(sem("norm_rt"), n + 1)
                dve.reciprocal(tiny[:, 6:8], tiny[:, 4:6]).then_inc(sem("norm_r"), 1)
                dve.wait_ge(sem("norm_r"), n + 1)
                TS(scratch[:, 0, :], src[:, 0, :], tiny[:, 6:7], None, ALU.mult).then_inc(sem("norm_xn0"), 1)

            def norm_end(n, dst, gain):
                for i in range(KC // 2):
                    dve.wait_ge(sem("norm_hi"), KC * n + 2 * i + 2)
                    for k in range(2):
                        kc = 2 * i + k
                        STT(dst[:, kc, 1, :], ps[:, ATT + i % 4, k * T:(k + 1) * T], col(gain, kc),
                            dst[:, kc, 0, :].bitcast(F32), ALU.mult, ALU.subtract).then_inc(sem("norm_lo"), 1)

            dve.memset(ones8[:], 1.0).then_inc(sem("ones"), 1)
            dve.memset(q_early[:], 0.0).then_inc(sem("ones"), 1)
            dve.memset(k_late[:], 0.0).then_inc(sem("ones"), 1)
            dve.wait_ge(sem("ones"), 3)
            dve.memset(q_early[:, 0:CHUNK], 1.0).then_inc(sem("ones"), 1)
            dve.memset(k_late[:, CHUNK:2 * CHUNK], -1e30).then_inc(sem("ones"), 1)

            for g in range(SLOTS):
                dve.wait_ge(hi_made, g + 1)
                TTo(w_lo[:, g, :], w_raw[:, g, :], w_hi[:, g, :].bitcast(F32), ALU.subtract).then_inc(lo_made, 1)
                if g == 0:
                    norm_begin(0, x0_tok, x0_n)

            n = 0

            def step(ins):
                nonlocal n
                n += 1
                ins.then_inc(sem("rope_step"), 1)
                dve.wait_ge(sem("rope_step"), n)

            TWO_PI = 2 * np.pi
            c1 = 6.28125
            c2 = float(np.floor((TWO_PI - c1) * 2 ** 20) / 2 ** 20)
            c3 = float(TWO_PI - c1 - c2)
            BIG = 1.5 * 2.0 ** 23
            PI_IN = 3.1415925
            dve.wait_ge(sem("pos_landed"), 16)
            dve.wait_ge(sem("cols_landed"), 16)
            step(dve.tensor_copy(gq[:, 1, :], gq[:, 0, :].bitcast(I32)))
            step(TS(gq[:, 1, :], gq[:, 1, :], col("inv_freq"), None, ALU.mult))
            step(TS(gp[:], gq[:, 1, :], float(1.0 / TWO_PI), BIG, ALU.mult, ALU.add))
            step(TS(gp[:], gp[:], BIG, None, ALU.subtract))
            step(STT(gk[:, 0, :], gp[:], -c1, gq[:, 1, :], ALU.mult, ALU.add))
            step(STT(gk[:, 0, :], gp[:], -c2, gk[:, 0, :], ALU.mult, ALU.add))
            step(STT(gk[:, 0, :], gp[:], -c3, gk[:, 0, :], ALU.mult, ALU.add))
            step(TS(gp[:], gk[:, 0, :], float(np.pi / 2), -TWO_PI, ALU.is_gt, ALU.mult))
            step(STT(gk[:, 1, :], gk[:, 0, :], float(np.pi / 2), gp[:], ALU.add, ALU.add))
            step(TS(gk[:, 1, :], gk[:, 1, :], -PI_IN, PI_IN, ALU.max, ALU.min))
            TS(gk[:, 0, :], gk[:, 0, :], -PI_IN, PI_IN, ALU.max, ALU.min).then_inc(sem("angles"), 1)
            norm_end(0, u, "g_mix")

            pos = Pos(0)
            for c in range(N_NARROW):
                split(pos, c)
            dve.wait_ge(sem("kpx_made"), 2)
            TS(kpx[:, 1, :], kpx[:, 2, :], col("g_kn_pe", 0, slice(0, ROPE)), None, ALU.mult
               ).then_inc(sem("kpg_made"), 1)
            dve.wait_ge(sem("z8"), 2)
            TS(zf8[:], zf8[:], col("b_f", 0, slice(0, 8)), None, ALU.add).then_inc(sem("f_made"), 1)
            TS(zi8[:], zi8[:], col("b_i", 0, slice(0, 8)), None, ALU.add).then_inc(sem("i_made"), 1)
            for c in range(KPB):
                split(pos, G_QA + c)
                if c == 0:
                    dve.wait_ge(sem("ls_act"), 2)
                    TS(g8b[:], g8b[:], 1.0, None, ALU.add).then_inc(sem("e_plus"), 1)
                    TS(zf8[:], zf8[:], 0.0, None, ALU.min).then_inc(sem("f_min"), 1)
                if c == 2:
                    dve.wait_ge(sem("ls_act"), 3)
                    dve.wait_ge(sem("f_min"), 1)
                    TTo(zf8[:], zf8[:], g8a[:], ALU.subtract).then_inc(sem("gate"), 1)
                    dve.memset(g8b[:], 0.0).then_inc(sem("gate"), 1)
                    dve.wait_ge(sem("gate"), 2)
                    dve.tensor_tensor_scan(g8a[:], zf8[:], g8b[:], 0.0, ALU.add, ALU.add).then_inc(sem("gate"), 1)
                    dve.wait_ge(sem("gate"), 3)
                    TTo(zi8[:], zi8[:], g8a[:], ALU.subtract).then_inc(sem("gate"), 1)
                    dve.wait_ge(sem("gate"), 4)
                    dve.tensor_tensor_scan(ncm[:], zi8[:], zi8[:], 0.0, ALU.max, ALU.max).then_inc(sem("gate"), 1)
                    dve.wait_ge(sem("gate"), 5)
                    TTo(g8b[:], g8a[:], ncm[:], ALU.add).then_inc(sem("m_neg"), 1)
                    dve.wait_ge(sem("m_neg"), 1)
                    TS(ncm[:], ncm[:], -1.0, None, ALU.mult).then_inc(sem("gate"), 1)
                    dve.tensor_copy(g8a[:], zi8[:]).then_inc(sem("gate"), 1)
                    dve.wait_ge(sem("gate"), 7)
                if c == 3:
                    dve.wait_ge(sem("kp_rot"), 1)
                    dve.wait_ge(sem("tables"), 2)
                    TS(kpx[:, 0, :], ps[0:ROPE, ATT + 1, 0:T], EPS, None, ALU.add).then_inc(sem("kp_mv"), 1)
                    TTo(kpx[:, 2, :], ps[0:ROPE, ATT + 1, T:2 * T], sin_t[0:ROPE, :], ALU.mult
                        ).then_inc(sem("kp"), 1)
                    TTo(kpx[:, 1, :], kpx[:, 1, :], cos_t[0:ROPE, :], ALU.mult).then_inc(sem("kp"), 1)
                    dve.wait_ge(sem("kp"), 2)
                    TTo(kpx[:, 1, :], kpx[:, 1, :], kpx[:, 2, :], ALU.add).then_inc(sem("kp"), 1)
                    dve.wait_ge(sem("kp_rt"), 1)
                    dve.reciprocal(kpx[:, 0, :], kpx[:, 0, :]).then_inc(sem("kp"), 1)
                    dve.wait_ge(sem("kp"), 4)
                    TTo(kpe[0:ROPE, :], kpx[:, 1, :], kpx[:, 0, :], ALU.mult).then_inc(sem("kpe_made"), 1)

            def latent(i):
                dve.wait_ge(sem("lat_ss"), TT * (i + 1))
                TS(tiny[:, 12 + 2 * i:14 + 2 * i], tiny[:, 8 + 2 * i:10 + 2 * i], 1.0 / LORA, EPS, ALU.mult, ALU.add
                   ).then_inc(sem("lat_mv"), 1)
                dve.wait_ge(sem("lat_rt"), i + 1)
                dve.reciprocal(tiny[:, 20 + 2 * i:22 + 2 * i], tiny[:, 16 + 2 * i:18 + 2 * i]
                               ).then_inc(sem("lat_r"), 1)

            def latent_lo(i, dst, gain):
                for b in range(2):
                    dve.wait_ge(sem("lat_hi"), 4 * i + 2 * b + 2)
                    for k in range(2):
                        kc = 2 * b + k
                        STT(dst[:, kc, 1, :], ps[:, ATT + 2 + b, k * T:(k + 1) * T], col(gain, kc),
                            dst[:, kc, 0, :].bitcast(F32), ALU.mult, ALU.subtract).then_inc(sem("lat_lo"), 1)

            latent(0)
            for c in range(KPB):
                split(pos, G_KV + c)
                if c == 5:
                    latent_lo(0, qa_t, "g_qa")
            latent(1)
            latent_lo(1, kv_t, "g_kva")
            dve.memset(v_aug[:, :, :, ML_DV:DV1], 1.0).then_inc(sem("ya_lo"), 1)

            def mla_pass(pos, it, filler):
                split(pos, 0)
                split(pos, 1)
                dve.wait_ge(sem("sqq_made"), it + 1)
                TS(gq[:].rearrange("p h t -> p (h t)"), ps[:, ATT, :], col("g_qn_nope"), None, ALU.mult
                   ).then_inc(sem("gq_made"), 1)
                dve.wait_ge(sem("sqp_made"), it + 1)
                TS(gp[:], ps[:, ATT + 3, 0:T], col("g_qn_pe"), None, ALU.mult).then_inc(sem("gp_made"), 1)
                split(pos, 2)
                split(pos, 3)
                dve.wait_ge(sem("sqk_made"), it + 1)
                TS(gk[:].rearrange("p h t -> p (h t)"), ps[:, ATT + 1, :], col("g_kn_nope"), None, ALU.mult
                   ).then_inc(sem("gk_made"), 1)
                split(pos, 4)
                split(pos, 5)
                dve.wait_ge(sem("ms_q"), it + 1)
                TS(sq_q[:].rearrange("p h t -> p (h t)"), ps[:, ATT, :], EPS, None, ALU.add).then_inc(sem("mv_q"), 1)
                dve.wait_ge(sem("ms_p"), it + 1)
                TS(sq_p[:], ps[:, ATT + 3, 0:T], EPS, None, ALU.add).then_inc(sem("mv_p"), 1)
                dve.wait_ge(sem("ms_k"), it + 1)
                TS(sq_k[:].rearrange("p h t -> p (h t)"), ps[:, ATT + 1, :], EPS, None, ALU.add
                   ).then_inc(sem("mv_k"), 1)
                TTo(pr[:, 0, 0:T], ps[:, ATT + 3, T:2 * T], sin_t[:], ALU.mult).then_inc(sem("rp"), 1)
                TTo(gp[:], gp[:], cos_t[:], ALU.mult).then_inc(sem("rp"), 1)
                dve.wait_ge(sem("rp"), 5 * it + 2)
                TTo(gp[:], gp[:], pr[:, 0, 0:T], ALU.add).then_inc(sem("rp"), 1)
                dve.wait_ge(sem("rt_q"), it + 1)
                dve.reciprocal(sq_q[:], sq_q[:]).then_inc(sem("rc"), 1)
                dve.wait_ge(sem("rt_p"), it + 1)
                dve.reciprocal(sq_p[:], sq_p[:]).then_inc(sem("rc"), 1)
                dve.wait_ge(sem("rt_k"), it + 1)
                dve.reciprocal(sq_k[:], sq_k[:]).then_inc(sem("rc"), 1)
                dve.wait_ge(sem("rc"), 3 * it + 3)
                dve.wait_ge(sem("rp"), 5 * it + 3)
                TTo(gq[:], gq[:], sq_q[:], ALU.mult).then_inc(sem("rp"), 1)
                TTo(gk[:], gk[:], sq_k[:], ALU.mult).then_inc(sem("rp"), 1)
                TTo(gp[:], gp[:], sq_p[:], ALU.mult).then_inc(sem("qk_ready"), 1)
                split(pos, 6)
                split(pos, 7)
                for h in range(2):
                    dve.wait_ge(sem("scored"), 2 * it + (h + 1))
                    for t in range(TT):
                        k = 2 * h + t
                        dve.tensor_reduce(tiny[:, 24 + k:25 + k], ps[:, ATT + h, t * P:t * P + (t + 1) * P], AX_X,
                                          ALU.max).then_inc(sem("row_max"), 1)
                dve.wait_ge(sem("row_max"), 4 * it + 4)
                TS(tiny[:, 28:32], tiny[:, 24:28], -MLA_SCALE, None, ALU.mult).then_inc(sem("neg_max"), 1)
                dve.wait_ge(sem("p_exp"), 4 * it + 4)
                dve.reciprocal(tiny[:, 36:40], tiny[:, 32:36]).then_inc(sem("p_rs"), 1)
                dve.wait_ge(sem("p_rs"), it + 1)
                for h in range(2):
                    for t in range(TT):
                        k = 2 * h + t
                        ins = TS(pr[:, h, t * P:t * P + (t + 1) * P], pr[:, h, t * P:t * P + (t + 1) * P],
                                 tiny[:, 36 + k:37 + k], None, ALU.mult)
                ins.then_inc(sem("p_ready"), 1)
                split(pos, 8)
                split(pos, 9)
                dve.wait_ge(sem("pT"), 2 * it + 2)
                dve.wait_ge(sem("pt_1"), it + 1)
                dve.tensor_copy(prt[:, 0, :], ps[:, ATT, 0:384]).then_inc(sem("pt_ready"), 2)
                split(pos, 10)
                split(pos, 11)
                if filler == "qk":
                    dve.wait_ge(sem("cv_first"), 4 * it + 4)
                    for tap in (2, 1, 0):
                        lag = 3 - tap
                        if tap < 2:
                            dve.wait_ge(sem("cv_taps"), 12 * it + 4 * (2 - tap))
                        for m in range(4):
                            dst = qk[:, bass.ds(4 * it + m, 1), lag:T].rearrange("p o t -> p (o t)")
                            STT(dst, ps[:, GEMM + m // 2, (m % 2) * T:(m % 2 + 1) * T - lag],
                                dcol("conv_qk", 16 * it + (4 * m + tap)), dst, ALU.mult, ALU.add
                                ).then_inc(sem("cv_taps"), 1)
                dve.wait_ge(sem("ya_hi"), it + 1)
                TTo(y_a[:, bass.ds(2 * it, 2), 1, :], ps[:, ATT + 2, :].rearrange("p (h t) -> p h t", h=2),
                    y_a[:, bass.ds(2 * it, 2), 0, :].bitcast(F32), ALU.subtract).then_inc(sem("ya_lo"), 1)

            with dve.Fori(0, 4) as j:
                mla_pass(Pos(G_MLA, j, MLA_PER), j, "qk")
            with dve.Fori(0, 4) as j:
                mla_pass(Pos(G_MLA + 4 * MLA_PER, j, MLA_PER), j + 4, "v")

            for c in range(KPB):
                split(Pos(G_ZO), c)

            dve.wait_ge(sem("attended"), PAIRS)
            with dve.Fori(0, NBLK) as j:
                pos = Pos(G_ML, j, KPB)
                for i in range(2):
                    TS(m_st[:, i, :], ncm[:], mats[0:8, bass.ds(2 * j + i, 1)], None, ALU.mult
                       ).then_inc(sem("m_staged"), 1)
                split(pos, 0)
                split(pos, 1)
                dve.wait_ge(sem("ml_scored"), j + 1)
                for i in range(2):
                    TS(w_ml[:, i, 0:T], ps[:, ATT + 2, i * T:(i + 1) * T],
                       a_tok[:, 0, bass.ds(2 * j + i, 1)], 0.0, ALU.add, ALU.min).then_inc(sem("ml_arg"), 1)
                    TS(w_ml[:, i, T:T + P], ps[:, ATT + 2, i * T + P:(i + 1) * T],
                       a_tok[:, 1, bass.ds(2 * j + i, 1)], 0.0, ALU.add, ALU.min).then_inc(sem("ml_arg"), 1)
                split(pos, 2)
                split(pos, 3)
                for i in range(2):
                    dve.wait_ge(sem("ml_w"), 2 * j + (i + 1))
                    for d in (0, T):
                        TTo(w_ml[:, i, d:d + P], w_ml[:, i, d:d + P], tri, ALU.mult).then_inc(sem("ml_tri"), 1)
                for i in range(2):
                    dve.wait_ge(sem("ml_tri"), 4 * j + 2 * (i + 1))
                    STT(w_ml[:, i, :], ps[:, ATT + i, 0:384], ML_SCALE, w_ml[:, i, :], ALU.mult, ALU.mult
                        ).then_inc(sem("ml_p"), 1)
                split(pos, 4)
                split(pos, 5)
                dve.wait_ge(sem("ml_num"), j + 1)
                for k in range(4):
                    dve.tensor_copy(tiny[:, 40 + k:41 + k], ps[:, ATT + k, ML_DV:DV1]).then_inc(sem("ml_den"), 1)
                dve.wait_ge(sem("ml_den"), 6 * j + 4)
                STT(tiny[:, 56:60], tiny[:, 40:44], -1.0, tiny[:, 40:44], ALU.mult, ALU.max
                    ).then_inc(sem("ml_den"), 1)
                dve.wait_ge(sem("ml_den"), 6 * j + 5)
                TTo(tiny[:, 40:44].rearrange("p (i t) -> p i t", t=TT),
                    tiny[:, 56:60].rearrange("p (i t) -> p i t", t=TT),
                    e_tok[:, :, bass.ds(2 * j, 2)].rearrange("p t i -> p i t"), ALU.max).then_inc(sem("ml_den"), 1)
                dve.wait_ge(sem("ml_den"), 6 * j + 6)
                dve.reciprocal(tiny[:, 40:44], tiny[:, 40:44]).then_inc(sem("ml_rd"), 1)
                dve.wait_ge(sem("ml_rd"), j + 1)
                for i in range(2):
                    for t in range(TT):
                        k = 2 * i + t
                        TS(hn[:, i, t, :], ps[:, ATT + k, 0:ML_DV], tiny[:, 40 + k:41 + k], None, ALU.mult
                           ).then_inc(sem("ml_hn"), 1)
                dve.wait_ge(sem("ml_ss"), 4 * j + 4)
                TS(tiny[:, 48:52], tiny[:, 44:48], 1.0 / ML_DV, EPS, ALU.mult, ALU.add).then_inc(sem("ml_mv"), 1)
                dve.wait_ge(sem("ml_rt"), j + 1)
                dve.reciprocal(tiny[:, 52:56], tiny[:, 48:52]).then_inc(sem("ml_rr"), 1)
                dve.wait_ge(sem("ml_rr"), j + 1)
                dve.wait_ge(sem("sig_made"), TT * j + TT)
                for i in range(2):
                    for t in range(TT):
                        k = 2 * i + t
                        STT(hn[:, i, t, :], hn[:, i, t, :], tiny[:, 52 + k:53 + k],
                            sig[:, t, i * ML_DV:(i + 1) * ML_DV], ALU.mult, ALU.mult).then_inc(sem("yb_tok"), 1)
                split(pos, 6)
                split(pos, 7)
                for i in range(2):
                    dve.wait_ge(sem("yb_hi"), 4 * j + 2 * (i + 1))
                    for half in range(2):
                        k = 2 * i + half
                        STT(y_b[:, bass.ds(4 * j + k, 1), 1, :].rearrange("p o t -> p (o t)"),
                            ps[:, ATT + i, half * T:(half + 1) * T], dcol("g_hnorm", 4 * j + k),
                            y_b[:, bass.ds(4 * j + k, 1), 0, :].bitcast(F32).rearrange("p o t -> p (o t)"),
                            ALU.mult, ALU.subtract).then_inc(sem("yb_lo"), 1)

            def merge_pass(pos, it, last):
                for c in range(KPB):
                    split(pos, c)
                dve.wait_ge(sem("sig_made"), TT * (NBLK + 1) + TT * it)
                for t in range(TT):
                    TTo(mg_a[:, t, :], ps[:, GEMM + t, :], sig[:, t, :], ALU.mult).then_inc(sem("mga"), 1)
                for c in range(KPB, 3 * KPB):
                    split(pos, c)
                dve.wait_ge(sem("sgb_made"), TT * it + TT)
                for t in range(TT):
                    TTo(mg[:, t, :], ps[:, ATT + t, :], sgb[:, t, :], ALU.mult).then_inc(sem("mgb_read"), 1)
                dve.wait_ge(sem("mgb_read"), TT * it + TT)
                dve.wait_ge(sem("mga"), TT * it + TT)
                TTo(mg[:], mg[:], mg_a[:], ALU.add).then_inc(sem("mg_made"), 1)
                if not last:
                    for c in range(3 * KPB, 3 * KPB + 4):
                        split(pos, c)
                for b in range(2):
                    dve.wait_ge(sem("mg_hi"), 2 * it + (b + 1))
                    TTo(mg_t[:, bass.ds(4 * it + 2 * b, 2), 1, :],
                        ps[:, GEMM + b, :].rearrange("p (k t) -> p k t", k=2),
                        mg_t[:, bass.ds(4 * it + 2 * b, 2), 0, :].bitcast(F32), ALU.subtract
                        ).then_inc(sem("mg_lo"), 1)
                if not last:
                    for c in range(3 * KPB + 4, 4 * KPB):
                        split(pos, c)

            with dve.Fori(0, NBLK - 1) as j:
                merge_pass(Pos(G_MERGE, j, 4 * KPB), j, False)
            merge_pass(Pos(G_MERGE + 4 * KPB * (NBLK - 1)), NBLK - 1, True)

            def wout_block(pos, it, bank):
                for c in range(KPB):
                    split(pos, c)
                dve.wait_ge(w_used, pos.n(KPB))
                for t in range(TT):
                    xs = (x_tok[:, t, it * BLK:(it + 1) * BLK] if isinstance(it, int)
                          else x_tok[:, t, bass.ds(it * BLK, BLK)])
                    TTo(xs, ps[:, bank + t, :], xs, ALU.add).then_inc(sem("x1_made"), 1)

            dve.wait_ge(sem("x_again0"), 16)
            dve.wait_ge(sem("x_again1"), 16)
            wout_block(Pos(G_WOUT), 0, GEMM)
            norm_begin(1, mem_tok, mem_n)
            for n in range(1, NBLK):
                wout_block(Pos(G_WOUT + n * KPB), n, GEMM + 2 * (n % 2))
            norm_end(1, mem_t, "g_mem")

            norm_begin(2, x_tok, xn)
            for c in range(KPB):
                split(Pos(G_CK), c)

            def c_gain(n, dst, gain):
                dve.wait_ge(sem("c_sqd"), 2 * n + 2)
                for b in range(2):
                    ins = TS(dst[:, 2 * b:2 * b + 2, :], ps[:, GEMM + b, :].rearrange("p (h t) -> p h t", h=2),
                             col(gain), None, ALU.mult)
                ins.then_inc(sem("c_g"), 1)

            def c_norm(n, dst):
                dve.wait_ge(sem("c_ms"), n + 1)
                for b in range(2):
                    TS(c_sq[:, 2 * b:2 * b + 2, :], ps[:, ATT + b, :].rearrange("p (h t) -> p h t", h=2), EPS, None,
                       ALU.add).then_inc(sem("c_mv"), 1)
                dve.wait_ge(sem("c_rt"), n + 1)
                dve.reciprocal(c_sq[:], c_sq[:]).then_inc(sem("c_rc"), 1)
                dve.wait_ge(sem("c_rc"), n + 1)
                dve.wait_ge(sem("c_g"), n + 1)
                TTo(dst[:], dst[:], c_sq[:], ALU.mult).then_inc(sem("c_ready"), 1)

            c_gain(0, ck, "g_ck")
            for c in range(KPB):
                split(Pos(G_CV), c)
            norm_end(2, u, "g_cross")
            c_norm(0, ck)
            for c in range(KPB):
                split(Pos(G_CQ), c)
            c_gain(1, cq, "g_cq")
            c_norm(1, cq)
            for h in range(CROSS_HEADS):
                dve.wait_ge(sem("c_scored"), h + 1)
                dve.tensor_reduce(tiny[:, 24 + 2 * h:26 + 2 * h],
                                  ps[:, ATT + h, :].rearrange("p (t k) -> p t k", t=TT), AX_X, ALU.max
                                  ).then_inc(sem("c_max"), 1)
                dve.wait_ge(sem("c_max"), h + 1)
                TS(tiny[:, 8 + 2 * h:10 + 2 * h], tiny[:, 24 + 2 * h:26 + 2 * h], -CROSS_SCALE, None, ALU.mult
                   ).then_inc(sem("c_nmax"), 1)
            for h in range(CROSS_HEADS):
                dve.wait_ge(sem("c_exp"), 2 * h + 2)
                dve.reciprocal(tiny[:, 32 + 2 * h:34 + 2 * h], tiny[:, 16 + 2 * h:18 + 2 * h]
                               ).then_inc(sem("c_rs"), 1)
                dve.wait_ge(sem("c_rs"), h + 1)
                for t in range(TT):
                    k = 32 + 2 * h + t
                    ins = TS(c_p[:, h, t, :], c_p[:, h, t, :], tiny[:, k:k + 1], None, ALU.mult)
                ins.then_inc(sem("c_p_ready"), 1)
            for b in range(2):
                dve.wait_ge(sem("yc_hi"), b + 1)
                TTo(yc[:, 2 * b:2 * b + 2, 1, :], ps[:, GEMM + b, :].rearrange("p (h t) -> p h t", h=2),
                    yc[:, 2 * b:2 * b + 2, 0, :].bitcast(F32), ALU.subtract).then_inc(sem("yc_lo"), 1)
            for n in range(NBLK):
                for c in range(2):
                    split(Pos(G_WO), 2 * n + c)
                dve.wait_ge(w_used, G_WO + 2 * n + 2)
                for t in range(TT):
                    xs = x_tok[:, t, n * BLK:(n + 1) * BLK]
                    TTo(xs, ps[:, 2 * n + t, :], xs, ALU.add).then_inc(sem("x2_made"), 1)
            norm_begin(3, x_tok, xn)
            norm_end(3, u, "g_ffn")

            with dve.Fori(0, UP_ITER) as j:
                pos = Pos(G_UP, j, UP_PER)
                for half, dst, pre in ((0, ua, "fa"), (1, ub, "fb")):
                    for c in range(KPB):
                        split(pos, half * KPB + c)
                    dve.wait_ge(sem(pre + "_first"), 4 * j + 4)
                    for tap in (1, 0):
                        lag = 2 - tap
                        if tap == 0:
                            dve.wait_ge(sem(pre + "_taps"), 8 * j + 4)
                        for m in range(4):
                            STT(dst[:, m, lag:T], ps[:, GEMM + 2 * half + m // 2, (m % 2) * T:(m % 2 + 1) * T - lag],
                                dcol("conv_ffn", 16 * j + (half * FC * 4 + 4 * m + tap)), dst[:, m, lag:T],
                                ALU.mult, ALU.add).then_inc(sem(pre + "_taps"), 1)
                dve.wait_ge(sem("fb_taps"), 8 * j + 8)
                dve.wait_ge(sem("fa_silu"), j + 1)
                TTo(h_ff[:, bass.ds(4 * j, 4), :], ua[:], ub[:], ALU.mult).then_inc(sem("h_made"), 1)

            def stage(it, kc):
                src = (h_ff[:, 4 * it + kc:4 * it + kc + 1, :] if isinstance(it, int)
                       else h_ff[:, bass.ds(4 * it + kc, 1), :])
                dve.wait_ge(sem("hst_hi"), 4 * it + (kc + 1))
                TTo(h_st[:, kc:kc + 1, 1, :], src, h_st[:, kc:kc + 1, 0, :].bitcast(F32), ALU.subtract
                    ).then_inc(sem("hst_lo"), 1)

            dve.wait_ge(sem("h_made"), UP_ITER)
            for kc in range(4):
                stage(0, kc)

            def down_pass(pos, it, last):
                for c in range(DOWN_PER):
                    split(pos, c)
                    if c % 2 and not last:
                        stage(it + 1, c // 2)

            with dve.Fori(0, DOWN_ITER - 1) as j:
                down_pass(Pos(G_DOWN, j, DOWN_PER), j, False)
            down_pass(Pos(G_DOWN + DOWN_PER * (DOWN_ITER - 1)), DOWN_ITER - 1, True)
            for n in range(NBLK):
                dve.wait_ge(w_used, G_END - 1 + n // 2)
                for t in range(TT):
                    xs = x_tok[:, t, n * BLK:(n + 1) * BLK]
                    TTo(xs, ps[:, t * 4 + n, :], xs, ALU.add).then_inc(sem("out_made"), 1)


def lay_out(i):
    f = np.float32
    w_in = np.asarray(i["w_in"])[0]
    at = np.cumsum([0, 512, 512, 64, 1024, 1024, 2048, 8, 8, 2048, 2048, 2048])
    qa0, kv0, kp0, q0, k0, v0, i0, f0, o0, ga0, gb0 = (int(a) for a in at[:-1])
    chunks = []

    def block(w, n0, width=BLK, rows=None):
        kk = w.shape[0] // P
        b = w[:, n0:n0 + width].reshape(kk // 2, 2, P, width).transpose(0, 2, 1, 3)
        chunks.append(b.reshape(kk // 2, P, 2 * width))

    narrow = np.zeros((D, P), f)
    narrow[:, 0:64] = w_in[:, kp0:kp0 + 64]
    narrow[:, 64:72] = w_in[:, i0:i0 + 8]
    narrow[:, 96:104] = w_in[:, f0:f0 + 8]
    chunks.append(narrow.reshape(2, 8, P, P).transpose(0, 2, 1, 3).reshape(2, P, 1024))
    block(w_in, qa0)
    block(w_in, kv0)
    wq = np.asarray(i["w_qb"])[0].reshape(LORA, PAIRS, 2, NOPE + ROPE)
    wkv = np.asarray(i["w_kvb"])[0].reshape(LORA, PAIRS, 2, 2, P)
    fill = [q0, q0 + BLK, k0, k0 + BLK] + [v0 + n * BLK for n in range(4)]
    for pair in range(PAIRS):
        b = np.zeros((LORA, BLK), f)
        b[:, 0:256] = wq[:, pair, :, 0:NOPE].reshape(LORA, 256)
        b[:, 256:384] = wq[:, pair, :, NOPE:].reshape(LORA, 128)
        block(b, 0)
        block(wkv[:, pair].transpose(0, 2, 1, 3).reshape(LORA, BLK), 0)
        block(w_in, fill[pair])
    for n in range(4):
        block(w_in, o0 + n * BLK)
    block(w_in, ga0)
    p_a, p_b, w_out = (np.asarray(i[n])[0] for n in ("p_a", "p_b", "w_out"))
    for n in range(4):
        block(p_a, n * BLK)
        block(w_in, gb0 + n * BLK)
        block(p_b, n * BLK)
        if n < 3:
            block(w_in, ga0 + (n + 1) * BLK)
    for n in range(4):
        block(w_out, n * BLK)
    for name in ("wk_c", "wv_c", "wq_c"):
        block(np.asarray(i[name])[0], 0)
    wo = np.asarray(i["wo_c"])[0]
    for n in range(4):
        block(wo, n * BLK)
    w_up = np.asarray(i["w_up"])[0]
    for n in range(UP_ITER):
        block(w_up, n * BLK)
        block(w_up, D_FF + n * BLK)
    w_down = np.asarray(i["w_down"])[0]
    chunks.append(w_down.reshape(FC, P, 2, 1024).transpose(0, 2, 1, 3).reshape(2 * FC, P, 1024))
    stream = np.concatenate(chunks)
    assert stream.shape[0] == G_END

    cols = np.zeros((P, NCOLS), f)

    def put(name, v, n=1):
        cols[:v.shape[0], COLS[name]:COLS[name] + n] = v.reshape(v.shape[0], n)

    for name in ("g_mix", "g_mem", "g_cross", "g_ffn"):
        put(name, np.asarray(i[name])[0].reshape(KC, P).T, KC)
    put("g_hnorm", np.asarray(i["g_hnorm"])[0].reshape(KC, P).T, KC)
    for name in ("g_qa", "g_kva"):
        put(name, np.asarray(i[name])[0].reshape(LC, P).T, LC)
    for name in ("g_qn_nope", "g_kn_nope", "g_cq", "g_ck"):
        put(name, np.asarray(i[name])[0])
    for name in ("g_qn_pe", "g_kn_pe"):
        put(name, np.tile(np.asarray(i[name])[0], 2))
    inv = f(ROPE_BASE) ** (-np.arange(0, ROPE, 2, dtype=f) / f(ROPE))
    put("inv_freq", np.tile(inv.astype(f), 4))
    put("b_i", np.asarray(i["b_if"])[0][0:8])
    put("b_f", np.asarray(i["b_if"])[0][8:16])
    put("conv_qk", np.asarray(i["conv_qk"])[0].reshape(4, 16, P).transpose(2, 1, 0), 64)
    ffn = np.zeros((P, 2 * FC, 4), f)
    ffn[:, :, 0:3] = np.asarray(i["conv_ffn"])[0].reshape(3, 2 * FC, P).transpose(2, 1, 0)
    ffn[:, :, 3] = np.asarray(i["b_conv_ffn"])[0].reshape(2 * FC, P).T
    put("conv_ffn", ffn, 2 * FC * 4)

    mats = np.zeros((P, 5 * P), f)
    mats[:, 0:P] = np.eye(P)
    for h in range(2):
        for a in range(ROPE // 2):
            lo, hi = h * ROPE + a, h * ROPE + a + ROPE // 2
            mats[hi, P + lo] = -1.0
            mats[lo, P + hi] = 1.0
    mats[:, 2 * P:3 * P] = 1.0 / P
    for h in range(2):
        mats[h * ROPE:(h + 1) * ROPE, 3 * P + h * ROPE:3 * P + (h + 1) * ROPE] = 1.0 / ROPE
    mats[:, 4 * P:5 * P] = np.triu(np.ones((P, P), f))
    return {
        "x": np.asarray(i["x"])[0], "mem": np.asarray(i["mem"])[0], "positions": np.asarray(i["positions"])[0],
        "cols": cols, "mats": mats, "stream": stream,
    }


def kernel(**inputs):
    import concourse.bacc as bacc
    from concourse.bass_utils import run_bass_kernel_spmd

    nc = bacc.Bacc("TRN2", target_bir_lowering=False, num_devices=1)
    arrays, args = {}, []
    for name, a in lay_out(inputs).items():
        a = np.ascontiguousarray(a)
        arrays[f"in_{name}"] = a
        args.append(nc.dram_tensor(f"in_{name}", a.shape, mybir.dt.from_np(a.dtype), kind="ExternalInput").ap())
    out = nc.dram_tensor("out", (T, D), F32, kind="ExternalOutput").ap()
    build(nc, *args, out)
    r = run_bass_kernel_spmd(nc, [arrays], core_ids=[0])
    return np.asarray(r.results[0]["out"]).reshape(1, T, D)
```

```python
import math

import numpy as np
from contextlib import ExitStack

import concourse.bass as bass
from concourse import mybir

F32 = mybir.dt.float32
F32R = mybir.dt.float32r
BF16 = mybir.dt.bfloat16
I32 = mybir.dt.int32
ALU = mybir.AluOpType
ACT = mybir.ActivationFunctionType
AX_X = mybir.AxisListType.X

P = 128
D = 2048
T = 256
TT = T // P
KC = D // P
HALF_ROOT = math.sqrt(0.5)
EPS = 1e-6
LORA = 512
LC = LORA // P
MLA_HEADS = 16
PAIRS = MLA_HEADS // 2
NOPE, ROPE = 128, 64
ROPE_BASE = 10000.0
MLA_SCALE = float(NOPE + ROPE) ** -0.5
ML_HEADS, ML_DK, ML_DV = 8, 128, 256
ML_SCALE = float(ML_DK) ** -0.5
CROSS_HEADS = 4
CROSS_SCALE = 128.0 ** -0.5
D_FF = 5632
FC = D_FF // P
CHUNK = 64
BLK = 512
NBLK = D // BLK
KPB = KC // 2

SLOTS = 4
N_NARROW = 2
G_QA = N_NARROW
G_KV = G_QA + KPB
G_MLA = G_KV + KPB
MLA_PER = 2 + 2 + KPB
G_ZO = G_MLA + PAIRS * MLA_PER
G_ML = G_ZO + KPB
G_MERGE = G_ML + NBLK * KPB
G_WOUT = G_MERGE + 4 * NBLK * KPB - KPB
G_CK = G_WOUT + NBLK * KPB
G_CQ = G_CK + KPB
G_CV = G_CQ + KPB
G_WO = G_CV + KPB
G_UP = G_WO + NBLK * 2
UP_ITER = D_FF // BLK
UP_PER = 2 * KPB
G_DOWN = G_UP + UP_ITER * UP_PER
DOWN_PER = 8
DOWN_ITER = FC * 2 // DOWN_PER
G_END = G_DOWN + FC * 2

COLS = {}
_at = 0
for _name, _n in (("g_mix", KC), ("g_mem", KC), ("g_cross", KC), ("g_ffn", KC), ("g_qa", LC), ("g_kva", LC),
                  ("g_hnorm", KC), ("g_qn_nope", 1), ("g_kn_nope", 1), ("g_qn_pe", 1), ("g_kn_pe", 1),
                  ("g_cq", 1), ("g_ck", 1), ("inv_freq", 1), ("b_i", 1), ("b_f", 1),
                  ("conv_qk", 64), ("conv_ffn", 2 * FC * 4), ("eps", 1)):
    COLS[_name] = _at
    _at += _n
NCOLS = _at


class Pos:

    def __init__(self, base, j=0, per=0):
        self.base, self.j, self.per = base, j, per

    def n(self, c):
        return self.base + c if self.per == 0 else self.per * self.j + (self.base + c)

    def slot(self, c):
        return (self.base + c) % SLOTS

    def landed(self, c):
        uses = (self.base + c) // SLOTS + 1
        return 16 * uses if self.per == 0 else (16 * self.per // SLOTS) * self.j + 16 * uses


def build(nc, x, mem, positions, cols_d, mats_d, stream, out):
    ctx = ExitStack()
    with ctx:
        def sb(name, shape, dt=F32):
            return ctx.enter_context(nc.sbuf_tensor(name, shape, dt))

        made = {}

        def sem(name):
            if name not in made:
                made[name] = ctx.enter_context(nc.semaphore(name))
            return made[name]

        def region(name, nbytes, *plans):
            res = {}
            for plan in plans:
                with ExitStack() as s:
                    for tname, shape, dt in plan:
                        res[tname] = s.enter_context(nc.sbuf_tensor(tname, shape, dt))
            ctx.enter_context(nc.sbuf_tensor(name, [P, nbytes // 4], F32))
            return res

        cols = sb("cols", [P, NCOLS])
        mats = sb("mats", [P, 5 * P])
        ident, rot = mats[:, 0:P], mats[:, P:2 * P]
        mean_nope, mean_pe, tri = mats[:, 2 * P:3 * P], mats[:, 3 * P:4 * P], mats[:, 4 * P:5 * P]
        ones8 = sb("ones8", [8, P])
        q_early = sb("q_early", [1, P], BF16)
        k_late = sb("k_late", [1, P], BF16)
        tiny = sb("tiny", [P, 64])
        a_tok = sb("a_tok", [P, TT, 8])
        e_tok = sb("e_tok", [P, TT, 8])

        w_raw = sb("w_raw", [P, SLOTS, 1024])
        w_hi = sb("w_hi", [P, SLOTS, 1024], F32R)
        w_lo = sb("w_lo", [P, SLOTS, 1024], F32R)

        u = sb("u", [P, KC, 2, T], F32R)
        rb = region("rb_rc", 2 * 32768,
                    [("y_a", [P, KC, 2, T], F32R), ("y_b", [P, KC, 2, T], F32R)],
                    [("rb_pad", [P, 8192], F32), ("qa_t", [P, LC, 2, T], F32R), ("kv_t", [P, LC, 2, T], F32R)],
                    [("mem_t", [P, KC, 2, T], F32R), ("mem_tok", [P, TT, D], F32), ("mem_n", [P, TT, D], F32)],
                    [("rb_pad2", [P, 8192], F32), ("ck", [P, 4, T], F32), ("cv", [P, TT, BLK], F32),
                     ("cq", [P, 4, T], F32), ("c_sq", [P, 4, T], F32),
                     ("c_p", [P, 4, TT, T], F32), ("c_pt", [P, 4, TT, T], F32)],
                    [("h_ff", [P, FC, T], F32)])
        y_a, y_b, qa_t, kv_t, mem_t = rb["y_a"], rb["y_b"], rb["qa_t"], rb["kv_t"], rb["mem_t"]
        mem_tok, mem_n, ck, cv, cq, c_sq, c_p, c_pt, h_ff = (
            rb[n] for n in ("mem_tok", "mem_n", "ck", "cv", "cq", "c_sq", "c_p", "c_pt", "h_ff"))
        DV1 = ML_DV + 1
        zv_b = TT * ML_HEADS * DV1 * 4
        zz = region(
            "zz", 16448 + 16384 + 24 * 1024,
            [("x0_n", [P, TT, D], F32), ("x0_pad", [P, 16], F32), ("x0_tok", [P, TT, D], F32)],
            [("zv_pad", [P, zv_b // 4], F32), ("lat_tok", [P, 2, TT, LORA], F32), ("kpx", [ROPE, 3, T], F32),
             ("zi8", [8, T], F32), ("zf8", [8, T], F32), ("g8a", [8, T], F32), ("g8b", [8, T], F32)],
            [("v_aug", [P, TT, ML_HEADS, DV1], F32), ("qk", [P, 16, T], F32),
             ("cos_t", [P, T], F32), ("sin_t", [P, T], F32), ("kpe", [P, T], F32), ("ncm", [8, T], F32),
             ("gq", [P, 2, T], F32), ("gk", [P, 2, T], F32), ("gp", [P, T], F32),
             ("sq_q", [P, 2, T], F32), ("sq_k", [P, 2, T], F32), ("sq_p", [P, T], F32),
             ("v_pair", [P, TT, 2, P], F32), ("pr", [P, 2, 384], F32), ("prt", [P, 2, 384], F32)],
            [("mpad", [P, zv_b // 4 + 16 * T + 4 * T], F32),
             ("sig", [P, TT, BLK], F32), ("k_st", [P, 2, T], F32), ("m_st", [8, 2, T], F32),
             ("w_ml", [P, 2, 384], F32), ("hn", [P, 2, TT, T], F32), ("junk", [P, T], F32)],
            [("mg_t", [P, KC, 2, T], F32R), ("mg_pad", [P, (zv_b + 16384 + 4096 - 32768) // 4], F32),
             ("mg_sig", [P, TT, BLK], F32), ("sgb", [P, TT, BLK], F32), ("mg_a", [P, TT, BLK], F32),
             ("mg", [P, TT, BLK], F32)],
            [("xn", [P, TT, D], F32), ("yc", [P, 4, 2, T], F32R), ("x_pad", [P, 2048], F32),
             ("x_tok", [P, TT, D], F32)],
            [("ua", [P, 4, T], F32), ("ub", [P, 4, T], F32)],
            [("dpad", [P, 4096], F32), ("h_st", [P, 4, 2, T], F32R)])
        (x0_n, x0_tok, lat_tok, kpx, zi8, zf8, g8a, g8b, v_aug, qk, cos_t, sin_t, kpe, ncm, gq, gk, gp, sq_q, sq_k,
         sq_p, v_pair, pr, prt, sig, k_st, m_st, w_ml, hn, junk, mg_t, sgb, mg_a, mg, xn, yc, x_tok, ua, ub, h_st) = (
            zz[n] for n in ("x0_n", "x0_tok", "lat_tok", "kpx", "zi8", "zf8", "g8a", "g8b", "v_aug", "qk", "cos_t",
                            "sin_t", "kpe", "ncm", "gq", "gk", "gp", "sq_q", "sq_k", "sq_p", "v_pair", "pr", "prt",
                            "sig", "k_st", "m_st", "w_ml", "hn", "junk", "mg_t", "sgb", "mg_a", "mg", "xn", "yc",
                            "x_tok", "ua", "ub", "h_st"))
        pr_flat, prt_flat = (b[:].rearrange("p h t -> p (h t)") for b in (pr, prt))
        y2_q, y2_p = pr_flat[:, 0:BLK], pr_flat[:, BLK:BLK + T]
        y2_k, rope_2 = prt_flat[:, 0:BLK], prt_flat[:, BLK:BLK + T]
        ps = ctx.enter_context(nc.psum_tensor("ps", [P, 8, BLK], F32))
        GEMM, ATT = 0, 4

        landed = [sem(f"landed{i}") for i in range(SLOTS)]
        hi_made, lo_made, w_used = sem("hi_made"), sem("lo_made"), sem("w_used")

        def col(name, i=0, rows=slice(0, P)):
            c = COLS[name] + i
            return cols[rows, c:c + 1]

        def dcol(name, i):
            return cols[:, bass.ds(i + COLS[name], 1)] if not isinstance(i, int) else col(name, i)

        block = ctx.enter_context(nc.Block())

        @block.sync
        def _(sp):
            for t in range(TT):
                sp.dma_start(x0_tok[:, t, :], x[t * P:(t + 1) * P, :]).then_inc(sem(f"x_landed{t}"), 16)
            for g in range(SLOTS):
                sp.dma_start(w_raw[:, g, :], stream[g]).then_inc(landed[g], 16)
            turns = G_END // SLOTS - 1
            with sp.Fori(0, turns) as j:
                for g in range(SLOTS):
                    sp.wait_ge(lo_made, SLOTS * j + (g + 1))
                    sp.wait_ge(landed[g], 16)
                    sp.dma_start(w_raw[:, g, :],
                                 stream[bass.ds(SLOTS * j + (SLOTS + g), 1)].rearrange("o p n -> p (o n)")
                                 ).then_inc(landed[g], 16)
            for g in range(G_END - G_END % SLOTS, G_END):
                sp.wait_ge(lo_made, g - SLOTS + 1)
                sp.dma_start(w_raw[:, g % SLOTS, :], stream[g]).then_inc(landed[g % SLOTS], 16)
            for n in range(NBLK):
                for t in range(TT):
                    sp.wait_ge(sem("out_made"), n * TT + t + 1)
                    sp.dma_start(out[t * P:(t + 1) * P, n * BLK:(n + 1) * BLK],
                                 x_tok[:, t, n * BLK:(n + 1) * BLK]).then_inc(sem("stored"), 16)
            sp.wait_ge(sem("stored"), 16 * NBLK * TT)

        @block.gpsimd
        def _(pool):
            pool.dma_start(cols[:], cols_d).then_inc(sem("cols_landed"), 16)
            pool.dma_start(mats[:], mats_d).then_inc(sem("mats_landed"), 16)
            pool.dma_start(gq[:, 0, :].bitcast(I32), positions.partition_broadcast(P)).then_inc(sem("pos_landed"), 16)
            pool.wait_ge(sem("kpe_made"), 1)
            pool.dma_start(kpe[ROPE:2 * ROPE, :], kpe[0:ROPE, :]).then_inc(sem("kpe_copied"), 16)
            pool.wait_ge(w_used, G_WOUT)
            for t in range(TT):
                pool.dma_start(mem_tok[:, t, :], mem[t * P:(t + 1) * P, :]).then_inc(sem(f"mem_landed{t}"), 16)
            pool.wait_ge(sem("mg_lo"), 2 * NBLK)
            for t in range(TT):
                pool.dma_start(x_tok[:, t, :], x[t * P:(t + 1) * P, :]).then_inc(sem(f"x_again{t}"), 16)

        @block.tensor
        def _(pe):
            def by_tokens(pos, c, act, kc0, last_kc, banks):
                s = pos.slot(c)
                pe.wait_ge(lo_made, pos.n(c) + 1)
                for k in range(2):
                    kc = kc0 + k
                    for t in range(TT):
                        a_hi, a_lo = (act[:, kc, half, t * P:(t + 1) * P] for half in (0, 1))
                        b_hi, b_lo = (w[:, s, k * BLK:(k + 1) * BLK] for w in (w_hi, w_lo))
                        o = ps[:, banks + t, :]
                        pe.matmul(o, a_hi, b_hi, start=(kc == 0), stop=False)
                        pe.matmul(o, a_hi, b_lo, start=False, stop=False)
                        mm = pe.matmul(o, a_lo, b_hi, start=False, stop=(kc == last_kc))
                mm.then_inc(w_used, 1)

            def feature_tile(o, s, lo, hi, act, kc, first, last):
                a_hi, a_lo = act[:, kc, 0, :], act[:, kc, 1, :]
                pe.matmul(o, w_hi[:, s, lo:hi], a_hi, start=first, stop=False, skip_group_check=True)
                pe.matmul(o, w_hi[:, s, lo:hi], a_lo, start=False, stop=False, skip_group_check=True)
                return pe.matmul(o, w_lo[:, s, lo:hi], a_hi, start=False, stop=last, skip_group_check=True)

            def by_features(pos, c, act, kc0, banks):
                s = pos.slot(c)
                pe.wait_ge(lo_made, pos.n(c) + 1)
                for k in range(2):
                    kc = kc0 + k
                    for m in range(4):
                        o = ps[:, banks + m // 2, (m % 2) * T:(m % 2 + 1) * T]
                        mm = feature_tile(o, s, k * BLK + m * P, k * BLK + (m + 1) * P, act, kc,
                                          kc == 0 and m % 2 == 0, kc == KC - 1)
                mm.then_inc(w_used, 1)

            def transposed_pair(n, src, i):
                if i >= 4:
                    pe.wait_ge(sem("norm_lo"), KC * n + 2 * (i - 3))
                for k in range(2):
                    for t in range(TT):
                        kc = 2 * i + k
                        mm = pe.transpose(ps[:, ATT + i % 4, k * T + t * P:k * T + (t + 1) * P],
                                          src[:, t, kc * P:(kc + 1) * P], ident)
                mm.then_inc(sem("norm_T"), 1)

            def normed(n):
                pe.wait_ge(sem("norm_xn0"), n + 1)
                pe.wait_ge(sem("norm_xn1"), n + 1)

            pe.wait_ge(sem("mats_landed"), 16)
            normed(0)
            for i in range(KC // 2):
                transposed_pair(0, x0_n, i)
            pe.wait_ge(sem("norm_lo"), KC * 1)

            pos = Pos(0)
            for c in range(N_NARROW):
                pe.wait_ge(lo_made, c + 1)
                for k in range(8):
                    kc = 8 * c + k
                    mm = feature_tile(ps[:, ATT, 0:T], c, k * P, (k + 1) * P, u, kc, kc == 0, kc == KC - 1)
                mm.then_inc(w_used, 1)
            for c in range(KPB):
                by_tokens(pos, G_QA + c, u, 2 * c, KC - 1, GEMM)
                if c == 2:
                    pe.wait_ge(sem("kpx_made"), 2)
                    pe.matmul(ps[0:ROPE, ATT + 1, 0:T], mean_pe[0:ROPE, 0:ROPE], kpx[:, 0, :], start=True, stop=True)
                    pe.wait_ge(sem("kpg_made"), 1)
                    pe.matmul(ps[0:ROPE, ATT + 1, T:2 * T], rot[0:ROPE, 0:ROPE], kpx[:, 1, :], start=True, stop=True,
                              skip_group_check=True).then_inc(sem("kp_rot"), 1)

            def latent_T(i):
                pe.wait_ge(sem("lat_n"), TT * (i + 1))
                for b in range(2):
                    if i == 1 and b == 0:
                        pe.wait_ge(sem("lat_lo"), LC)
                    for k in range(2):
                        for t in range(TT):
                            kc = 2 * b + k
                            mm = pe.transpose(ps[:, ATT + 2 + b, k * T + t * P:k * T + (t + 1) * P],
                                              lat_tok[:, i, t, kc * P:(kc + 1) * P], ident)
                    mm.then_inc(sem("lat_T"), 1)

            for c in range(KPB):
                by_tokens(pos, G_KV + c, u, 2 * c, KC - 1, GEMM + 2)
                if c == 4:
                    latent_T(0)
                if c == 6:
                    pe.wait_ge(sem("gates_made"), 1)
                    for t in range(TT):
                        pe.transpose(ps[:, ATT, t * 8:t * 8 + 8], g8a[:, t * P:(t + 1) * P], ident[0:8, 0:8])
                    for t in range(TT):
                        mm = pe.transpose(ps[:, ATT, 16 + t * 8:24 + t * 8], g8b[:, t * P:(t + 1) * P],
                                          ident[0:8, 0:8])
                    mm.then_inc(sem("gates_T"), 1)
            latent_T(1)
            pe.wait_ge(sem("lat_lo"), 2 * LC)

            def mla_pass(pos, it, filler):
                def fill(i):
                    if filler == "qk":
                        by_features(pos, 4 + i, u, 2 * i, GEMM)
                    else:
                        by_tokens(pos, 4 + i, u, 2 * i, KC - 1, GEMM)

                A0, A1, A2, A3 = ATT, ATT + 1, ATT + 2, ATT + 3
                for c in range(2):
                    s = pos.slot(c)
                    pe.wait_ge(lo_made, pos.n(c) + 1)
                    for k in range(2):
                        kc = 2 * c + k
                        for h in range(2):
                            feature_tile(ps[:, A0, h * T:(h + 1) * T], s, k * BLK + h * P, k * BLK + (h + 1) * P,
                                         qa_t, kc, kc == 0 and h == 0, kc == LC - 1)
                        mm = feature_tile(ps[:, A3, 0:T], s, k * BLK + 2 * P, k * BLK + 3 * P, qa_t, kc, kc == 0,
                                          kc == LC - 1)
                    mm.then_inc(w_used, 1)
                pe.wait_ge(sem("ya_lo"), it + 1)
                for c in range(2, 4):
                    s = pos.slot(c)
                    pe.wait_ge(lo_made, pos.n(c) + 1)
                    for k in range(2):
                        kc = 2 * (c - 2) + k
                        for h in range(2):
                            feature_tile(ps[:, A1, h * T:(h + 1) * T], s, k * BLK + h * P, k * BLK + (h + 1) * P,
                                         kv_t, kc, kc == 0 and h == 0, kc == LC - 1)
                        for t in range(TT):
                            o = ps[:, A2, t * T:(t + 1) * T]
                            a_hi, a_lo = (kv_t[:, kc, half, t * P:(t + 1) * P] for half in (0, 1))
                            b_hi, b_lo = (w[:, s, k * BLK + T:(k + 1) * BLK] for w in (w_hi, w_lo))
                            pe.matmul(o, a_hi, b_hi, start=(kc == 0 and t == 0), stop=False, skip_group_check=True)
                            pe.matmul(o, a_hi, b_lo, start=False, stop=False, skip_group_check=True)
                            mm = pe.matmul(o, a_lo, b_hi, start=False, stop=(kc == LC - 1), skip_group_check=True)
                    mm.then_inc(w_used, 1)
                pe.wait_ge(sem("gq_made"), it + 1)
                pe.matmul(ps[:, A0, :], mean_nope, sq_q[:].rearrange("p h t -> p (h t)"), start=True, stop=True
                          ).then_inc(sem("ms_q"), 1)
                pe.wait_ge(sem("gp_made"), it + 1)
                pe.matmul(ps[:, A3, 0:T], mean_pe, sq_p[:], start=True, stop=True)
                pe.matmul(ps[:, A3, T:2 * T], rot, gp[:], start=True, stop=True, skip_group_check=True
                          ).then_inc(sem("ms_p"), 1)
                fill(0)
                pe.wait_ge(sem("gk_made"), it + 1)
                pe.matmul(ps[:, A1, :], mean_nope, sq_k[:].rearrange("p h t -> p (h t)"), start=True, stop=True
                          ).then_inc(sem("ms_k"), 1)
                fill(1)
                fill(2)
                fill(3)
                pe.wait_ge(sem("qk_ready"), it + 1)
                pe.wait_ge(sem("kpe_copied"), 16)
                for h in range(2):
                    rows = slice(h * ROPE, (h + 1) * ROPE)
                    for t in range(TT):
                        o = ps[:, A0 + h, t * P:t * P + (t + 1) * P]
                        q = slice(t * P, (t + 1) * P)
                        keys = slice(0, (t + 1) * P)
                        pe.matmul(o, gq[:, h, q], gk[:, h, keys], start=(t == 0), stop=False, skip_group_check=True)
                        pe.matmul(o, gp[rows, q], kpe[rows, keys], start=False, stop=False, skip_group_check=True)
                        diag = ps[:, A0 + h, 2 * t * P:(2 * t + 1) * P]
                        mm = pe.matmul(diag, q_early[:], k_late[:], start=False, stop=True, skip_group_check=True)
                    mm.then_inc(sem("scored"), 1)
                fill(4)
                fill(5)
                pe.wait_ge(sem("p_ready"), it + 1)
                for h in range(2):
                    for src, dst in ((0, 0), (1, 1), (2, 2)):
                        mm = pe.transpose(ps[:, A0 + h, dst * P:(dst + 1) * P], pr[:, h, src * P:(src + 1) * P], ident)
                    mm.then_inc(sem("pT"), 1)
                fill(6)
                fill(7)
                pe.wait_ge(sem("pt_ready"), 2 * it + 2)
                for h in range(2):
                    o = ps[:, A2, h * T:(h + 1) * T]
                    pe.matmul(o, v_pair[:, 0, h, :], prt[:, h, 0:T], start=(h == 0), stop=False,
                              skip_group_check=True)
                    mm = pe.matmul(ps[:, A2, h * T + P:(h + 1) * T], v_pair[:, 1, h, :], prt[:, h, T:T + P],
                                   start=False, stop=True, skip_group_check=True)
                mm.then_inc(sem("attended"), 1)

            with pe.Fori(0, 4) as j:
                mla_pass(Pos(G_MLA, j, MLA_PER), j, "qk")
            with pe.Fori(0, 4) as j:
                mla_pass(Pos(G_MLA + 4 * MLA_PER, j, MLA_PER), j + 4, "v")

            pe.wait_ge(sem("zv_read"), TT * 4)
            for c in range(KPB):
                by_tokens(Pos(G_ZO), c, u, 2 * c, KC - 1, GEMM + 2)

            def mlstm_pass(pos, j, bank):
                by_tokens(pos, 0, u, 0, KC - 1, bank)
                by_tokens(pos, 1, u, 2, KC - 1, bank)
                pe.wait_ge(sem("k_staged"), j + 1)
                pe.wait_ge(sem("m_staged"), 2 * j + 2)
                for i in range(2):
                    q_all = qk[:, bass.ds(2 * j + i, 1), :]
                    q_late = qk[:, bass.ds(2 * j + i, 1), P:T]
                    pe.matmul(ps[:, ATT + i, 0:T], k_st[:, i, 0:P], q_all, start=True, stop=True,
                              skip_group_check=True)
                    mm = pe.matmul(ps[:, ATT + i, T:T + P], k_st[:, i, P:T], q_late, start=True, stop=True,
                                   skip_group_check=True)
                mm = pe.matmul(ps[:, ATT + 2, :], ones8[:], m_st[:].rearrange("p h t -> p (h t)"), start=True,
                               stop=True).then_inc(sem("ml_scored"), 1)
                for c in (2, 3, 4):
                    by_tokens(pos, c, u, 2 * c, KC - 1, bank)
                pe.wait_ge(sem("ml_p"), 2 * j + 2)
                for i in range(2):
                    v0, v1 = (v_aug[:, t, bass.ds(2 * j + i, 1), :] for t in range(TT))
                    pe.matmul(ps[:, ATT + 2 * i, 0:DV1], w_ml[:, i, 0:P], v0, start=True, stop=True)
                    pe.matmul(ps[:, ATT + 2 * i + 1, 0:DV1], w_ml[:, i, P:T], v0, start=True, stop=False)
                    mm = pe.matmul(ps[:, ATT + 2 * i + 1, 0:DV1], w_ml[:, i, T:T + P], v1, start=False, stop=True)
                mm.then_inc(sem("ml_num"), 1)
                for c in (5, 6, 7):
                    by_tokens(pos, c, u, 2 * c, KC - 1, bank)
                pe.wait_ge(sem("yb_tok"), 4 * j + 4)
                for i in range(2):
                    for half in range(2):
                        for t in range(TT):
                            mm = pe.transpose(ps[:, ATT + i, half * T + t * P:half * T + (t + 1) * P],
                                              hn[:, i, t, half * P:(half + 1) * P], ident)
                    mm.then_inc(sem("yb_T"), 1)

            with pe.Fori(0, NBLK // 2) as j:
                for n in range(2):
                    mlstm_pass(Pos(G_ML + n * KPB, j, 2 * KPB), 2 * j + n, GEMM + 2 * n)

            def merge_pass(pos, it, last):
                for c in range(KPB):
                    by_tokens(pos, c, y_a, 2 * c, KC - 1, GEMM)
                for c in range(KPB):
                    by_tokens(pos, KPB + c, u, 2 * c, KC - 1, GEMM + 2)
                for c in range(KPB):
                    by_tokens(pos, 2 * KPB + c, y_b, 2 * c, KC - 1, ATT)
                if not last:
                    pe.wait_ge(sem("sig_made"), TT * (NBLK + 1) + TT * it)
                    for c in range(4):
                        by_tokens(pos, 3 * KPB + c, u, 2 * c, KC - 1, ATT + 2)
                else:
                    pe.wait_ge(sem("mg_lo"), 2 * (NBLK - 1))
                    for c in range(3):
                        by_tokens(Pos(G_WOUT), c, mg_t, 2 * c, KC - 1, GEMM + 2)
                pe.wait_ge(sem("mg_made"), it + 1)
                for b in range(2):
                    for k in range(2):
                        for t in range(TT):
                            kc = 2 * b + k
                            mm = pe.transpose(ps[:, GEMM + b, k * T + t * P:k * T + (t + 1) * P],
                                              mg[:, t, kc * P:(kc + 1) * P], ident)
                    mm.then_inc(sem("mg_T"), 1)
                if not last:
                    for c in range(4, KPB):
                        by_tokens(pos, 3 * KPB + c, u, 2 * c, KC - 1, ATT + 2)

            pe.wait_ge(sem("yb_lo"), 4 * NBLK)
            with pe.Fori(0, NBLK - 1) as j:
                merge_pass(Pos(G_MERGE, j, 4 * KPB), j, False)
            pe.wait_ge(sem("mg_lo"), 2 * (NBLK - 1))
            merge_pass(Pos(G_MERGE + 4 * KPB * (NBLK - 1)), NBLK - 1, True)

            for n in range(NBLK):
                if n == NBLK - 1:
                    normed(1)
                for c in range(3 if n == 0 else 0, KPB):
                    if n == 0 and c >= 6:
                        pe.wait_ge(sem("mg_lo"), 2 * (NBLK - 1) + c - 5)
                    by_tokens(Pos(G_WOUT + n * KPB), c, mg_t, 2 * c, KC - 1, GEMM + 2 * (1 - n % 2))
                    if n == NBLK - 1:
                        transposed_pair(1, mem_n, c)

            pe.wait_ge(sem("x1_made"), 2 * TT * 2)
            for c in range(KPB):
                pe.wait_ge(sem("norm_lo"), KC + 2 * (c + 1))
                by_features(Pos(G_CK), c, mem_t, 2 * c, GEMM)
                if c == 4:
                    normed(2)
                if c >= 4:
                    transposed_pair(2, xn, 2 * (c - 4))
                    transposed_pair(2, xn, 2 * (c - 4) + 1)

            def mean_squares(n):
                pe.wait_ge(sem("c_g"), n + 1)
                for b in range(2):
                    mm = pe.matmul(ps[:, ATT + b, :], mean_nope, c_sq[:, 2 * b:2 * b + 2, :], start=True, stop=True)
                mm.then_inc(sem("c_ms"), 1)

            for c in range(KPB):
                pe.wait_ge(sem("norm_lo"), KC * 2 + 2 * (c + 1))
                by_features(Pos(G_CQ), c, u, 2 * c, GEMM + 2)
                if c == 3:
                    pe.wait_ge(sem("norm_lo"), KC * 3)
                    mean_squares(0)
            for c in range(KPB):
                by_tokens(Pos(G_CV), c, mem_t, 2 * c, KC - 1, GEMM)
                if c == 0:
                    mean_squares(1)
                if c == 4:
                    pe.wait_ge(sem("c_ready"), 2)
                    for h in range(CROSS_HEADS):
                        for t in range(TT):
                            mm = pe.matmul(ps[:, ATT + h, t * T:(t + 1) * T], cq[:, h, t * P:(t + 1) * P],
                                           ck[:, h, :], start=True, stop=True, skip_group_check=True)
                        mm.then_inc(sem("c_scored"), 1)
                if c == 6:
                    for h in range(CROSS_HEADS):
                        pe.wait_ge(sem("c_p_ready"), h + 1)
                        for s in range(TT):
                            for t in range(TT):
                                mm = pe.transpose(ps[:, ATT + h, s * T + t * P:s * T + (t + 1) * P],
                                                  c_p[:, h, t, s * P:(s + 1) * P], ident)
                        mm.then_inc(sem("c_pT"), 1)
            pe.wait_ge(sem("cv_v"), TT)
            for h in range(CROSS_HEADS):
                pe.wait_ge(sem("c_pt_ready"), h + 1)
                o = ps[:, GEMM + 2 + h // 2, (h % 2) * T:(h % 2 + 1) * T]
                for s in range(TT):
                    mm = pe.matmul(o, cv[:, s, h * P:(h + 1) * P], c_pt[:, h, s, :], start=(s == 0), stop=(s == 1),
                                   skip_group_check=True)
                if h % 2:
                    mm.then_inc(sem("c_att"), 1)
            for n in range(NBLK):
                for c in range(2):
                    if n == 0:
                        pe.wait_ge(sem("yc_lo"), c + 1)
                    by_tokens(Pos(G_WO), 2 * n + c, yc, 2 * c, 3, 2 * n)

            def up_pass(pos, first):
                for c in range(KPB):
                    if first:
                        pe.wait_ge(sem("norm_lo"), KC * 3 + 2 * (c + 1))
                    by_features(pos, c, u, 2 * c, GEMM)
                    if first and c < 4:
                        transposed_pair(3, xn, 4 + c)
                for c in range(KPB):
                    by_features(pos, KPB + c, u, 2 * c, GEMM + 2)

            normed(3)
            for i in range(4):
                transposed_pair(3, xn, i)
            up_pass(Pos(G_UP), True)
            with pe.Fori(0, UP_ITER - 1) as j:
                up_pass(Pos(G_UP + UP_PER, j, UP_PER), False)

            def down_pass(pos, it, first, last):
                for c in range(DOWN_PER):
                    s, kc, half = pos.slot(c), c // 2, c % 2
                    if first and c < 2:
                        pe.wait_ge(sem(("fa_taps", "fb_taps")[c]), 8 * UP_ITER)
                    pe.wait_ge(lo_made, pos.n(c) + 1)
                    if half == 0:
                        pe.wait_ge(sem("hst_lo"), 4 * it + (kc + 1))
                    for t in range(TT):
                        a_hi, a_lo = (h_st[:, kc, hl, t * P:(t + 1) * P] for hl in (0, 1))
                        for n in range(2):
                            o = ps[:, t * 4 + half * 2 + n, :]
                            b_hi, b_lo = (w[:, s, n * BLK:(n + 1) * BLK] for w in (w_hi, w_lo))
                            pe.matmul(o, a_hi, b_hi, start=(first and kc == 0), stop=False, skip_group_check=True)
                            pe.matmul(o, a_hi, b_lo, start=False, stop=False, skip_group_check=True)
                            mm = pe.matmul(o, a_lo, b_hi, start=False, stop=(last and kc == 3),
                                           skip_group_check=True)
                    mm.then_inc(w_used, 1)

            down_pass(Pos(G_DOWN), 0, True, False)
            with pe.Fori(0, DOWN_ITER - 2) as j:
                down_pass(Pos(G_DOWN + DOWN_PER, j, DOWN_PER), j + 1, False, False)
            down_pass(Pos(G_DOWN + DOWN_PER * (DOWN_ITER - 1)), DOWN_ITER - 1, False, True)

        @block.scalar
        def _(act):
            def split(pos, c):
                if pos.per == 0 and pos.base + c + SLOTS >= G_END:
                    return
                s = pos.slot(c)
                act.wait_ge(landed[s], pos.landed(c + SLOTS))
                act.wait_ge(w_used, pos.n(c) + 1)
                act.activation(w_hi[:, s, :], w_raw[:, s, :], ACT.Copy).then_inc(hi_made, 1)

            def norm_begin(n, src, scratch, ready):
                for t in range(TT):
                    act.wait_ge(*ready[t])
                    act.activation(scratch[:, t, :], src[:, t, :], ACT.Square, accum_out=tiny[:, t:t + 1]
                                   ).then_inc(sem("norm_ss"), 1)
                norm_scale(n, src, scratch)

            def norm_scale(n, src, scratch):
                act.wait_ge(sem("norm_mv"), n + 1)
                act.activation(tiny[:, 4:6], tiny[:, 2:4], ACT.Sqrt).then_inc(sem("norm_rt"), 1)
                act.wait_ge(sem("norm_r"), n + 1)
                act.wait_ge(sem("norm_ss"), TT * min(n + 1, 3))
                act.activation(scratch[:, 1, :], src[:, 1, :], ACT.Copy, scale=tiny[:, 7:8]
                               ).then_inc(sem("norm_xn1"), 1)

            def norm_pair(n, dst, gain, i):
                act.wait_ge(sem("norm_T"), KC // 2 * n + i + 1)
                for k in range(2):
                    kc = 2 * i + k
                    act.activation(dst[:, kc, 0, :], ps[:, ATT + i % 4, k * T:(k + 1) * T], ACT.Copy,
                                   scale=col(gain, kc)).then_inc(sem("norm_hi"), 1)

            norm_begin(0, x0_tok, x0_n, [(sem("x_landed0"), 16), (sem("x_landed1"), 16)])
            for g in range(SLOTS):
                act.wait_ge(landed[g], 16)
                act.activation(w_hi[:, g, :], w_raw[:, g, :], ACT.Copy).then_inc(hi_made, 1)
                if g == 0:
                    act.wait_ge(sem("cols_landed"), 16)
                    for i in range(KC // 2):
                        norm_pair(0, u, "g_mix", i)
            act.wait_ge(sem("angles"), 1)
            act.activation(sin_t[:], gk[:, 0, :], ACT.Sin).then_inc(sem("tables"), 1)
            act.activation(cos_t[:], gk[:, 1, :], ACT.Sin).then_inc(sem("tables"), 1)
            pos = Pos(0)
            for c in range(N_NARROW):
                split(pos, c)
            act.activation(kpx[:, 2, :], ps[0:ROPE, ATT, 0:T], ACT.Copy).then_inc(sem("kpx_made"), 1)
            act.activation(kpx[:, 0, :], ps[0:ROPE, ATT, 0:T], ACT.Square).then_inc(sem("kpx_made"), 1)
            act.activation(zi8[:], ps[64:72, ATT, 0:T], ACT.Copy).then_inc(sem("z8"), 1)
            act.activation(zf8[:], ps[96:104, ATT, 0:T], ACT.Copy).then_inc(sem("z8"), 1)
            for c in range(KPB):
                split(pos, G_QA + c)
                if c == 0:
                    act.wait_ge(sem("f_made"), 1)
                    act.activation(g8a[:], zf8[:], ACT.Abs).then_inc(sem("ls_act"), 1)
                    act.wait_ge(sem("ls_act"), 1)
                    act.activation(g8b[:], g8a[:], ACT.Exp, scale=-1.0).then_inc(sem("ls_act"), 1)
                if c == 1:
                    act.wait_ge(sem("e_plus"), 1)
                    act.activation(g8a[:], g8b[:], ACT.Ln).then_inc(sem("ls_act"), 1)
                if c == 3:
                    act.wait_ge(sem("kp_rot"), 1)
                    act.wait_ge(sem("kp_mv"), 1)
                    act.activation(kpx[:, 0, :], kpx[:, 0, :], ACT.Sqrt).then_inc(sem("kp_rt"), 1)
                if c == 5:
                    act.wait_ge(sem("m_neg"), 1)
                    act.activation(g8b[:], g8b[:], ACT.Exp, scale=-1.0).then_inc(sem("gates_made"), 1)

            def latent(i, bank):
                for t in range(TT):
                    act.activation(lat_tok[:, i, t, :], ps[:, bank + t, :], ACT.Square,
                                   accum_out=tiny[:, 8 + 2 * i + t:9 + 2 * i + t]).then_inc(sem("lat_ss"), 1)
                act.wait_ge(sem("lat_mv"), i + 1)
                act.activation(tiny[:, 16 + 2 * i:18 + 2 * i], tiny[:, 12 + 2 * i:14 + 2 * i], ACT.Sqrt
                               ).then_inc(sem("lat_rt"), 1)
                act.wait_ge(sem("lat_r"), i + 1)
                act.wait_ge(sem("lat_ss"), TT * (i + 1))
                for t in range(TT):
                    act.activation(lat_tok[:, i, t, :], ps[:, bank + t, :], ACT.Copy,
                                   scale=tiny[:, 20 + 2 * i + t:21 + 2 * i + t]).then_inc(sem("lat_n"), 1)

            def latent_hi(i, dst, gain):
                for b in range(2):
                    act.wait_ge(sem("lat_T"), 2 * i + b + 1)
                    for k in range(2):
                        kc = 2 * b + k
                        act.activation(dst[:, kc, 0, :], ps[:, ATT + 2 + b, k * T:(k + 1) * T], ACT.Copy,
                                       scale=col(gain, kc)).then_inc(sem("lat_hi"), 1)

            latent(0, GEMM)
            for c in range(KPB):
                split(pos, G_KV + c)
                if c == 5:
                    latent_hi(0, qa_t, "g_qa")
                if c == 7:
                    act.wait_ge(sem("gates_T"), 1)
                    act.activation(a_tok[:].rearrange("p t h -> p (t h)"), ps[:, ATT, 0:16], ACT.Copy
                                   ).then_inc(sem("gates_tok"), 1)
                    act.activation(e_tok[:].rearrange("p t h -> p (t h)"), ps[:, ATT, 16:32], ACT.Copy
                                   ).then_inc(sem("gates_tok"), 1)
            latent(1, GEMM + 2)
            latent_hi(1, kv_t, "g_kva")

            def mla_pass(pos, it, filler):
                split(pos, 0)
                split(pos, 1)
                act.activation(sq_q[:].rearrange("p h t -> p (h t)"), ps[:, ATT, :], ACT.Square
                               ).then_inc(sem("sqq_made"), 1)
                act.activation(sq_p[:], ps[:, ATT + 3, 0:T], ACT.Square).then_inc(sem("sqp_made"), 1)
                split(pos, 2)
                split(pos, 3)
                act.activation(sq_k[:].rearrange("p h t -> p (h t)"), ps[:, ATT + 1, :], ACT.Square
                               ).then_inc(sem("sqk_made"), 1)
                act.activation(v_pair[:].rearrange("p t h d -> p (t h d)"), ps[:, ATT + 2, :], ACT.Copy
                               ).then_inc(sem("v_made"), 1)
                eps = col("eps")
                yq, yk = (b[:].rearrange("p h t -> p (h t)") for b in (sq_q, sq_k))
                inv = sem("inv_rms")
                act.preload_act_table_set("natural_log_exp_and_others")
                act.wait_ge(sem("ms_q"), it + 1)
                act.activation(yq, ps[:, ATT, :], ACT.Ln, bias=eps).then_inc(inv, 1)
                act.wait_ge(sem("ms_p"), it + 1)
                act.activation(sq_p[:], ps[:, ATT + 3, 0:T], ACT.Ln, bias=eps).then_inc(inv, 1)
                act.wait_ge(inv, 9 * it + 1)
                act.activation(yq, yq, ACT.Exp, scale=-0.5).then_inc(inv, 1)
                act.wait_ge(inv, 9 * it + 2)
                act.activation(sq_p[:], sq_p[:], ACT.Exp, scale=-0.5).then_inc(inv, 1)
                act.wait_ge(inv, 9 * it + 3)
                act.activation(y2_q, yq, ACT.Square, scale=HALF_ROOT).then_inc(inv, 1)
                act.wait_ge(inv, 9 * it + 4)
                act.activation(y2_p, sq_p[:], ACT.Square, scale=HALF_ROOT).then_inc(inv, 1)
                split(pos, 4)
                act.wait_ge(sem("ms_k"), it + 1)
                act.activation(yk, ps[:, ATT + 1, :], ACT.Ln, bias=eps).then_inc(inv, 1)
                act.wait_ge(inv, 9 * it + 7)
                act.activation(yk, yk, ACT.Exp, scale=-0.5).then_inc(inv, 1)
                act.wait_ge(inv, 9 * it + 8)
                act.activation(y2_k, yk, ACT.Square, scale=HALF_ROOT).then_inc(inv, 1)
                split(pos, 5)
                split(pos, 6)
                split(pos, 7)
                act.wait_ge(sem("neg_max"), it + 1)
                for h in range(2):
                    for t in range(TT):
                        n = 2 * h + t
                        act.activation(pr[:, h, t * P:t * P + (t + 1) * P],
                                       ps[:, ATT + h, t * P:t * P + (t + 1) * P], ACT.Exp,
                                       bias=tiny[:, 28 + n:29 + n], scale=MLA_SCALE,
                                       accum_out=tiny[:, 32 + n:33 + n]).then_inc(sem("p_exp"), 1)
                split(pos, 8)
                split(pos, 9)
                act.wait_ge(sem("pT"), 2 * it + 2)
                act.activation(prt[:, 1, :], ps[:, ATT + 1, 0:384], ACT.Copy).then_inc(sem("pt_1"), 1)
                if filler == "v":
                    act.wait_ge(sem("cv_taps"), 48)
                    silu = qk[:, bass.ds(4 * (it - 4), 4), :]
                    act.activation(silu, silu, ACT.Silu).then_inc(sem("cv_made"), 1)
                split(pos, 10)
                split(pos, 11)
                if filler == "qk":
                    for m in range(4):
                        act.activation(qk[:, bass.ds(4 * it + m, 1), :],
                                       ps[:, GEMM + m // 2, (m % 2) * T:(m % 2 + 1) * T], ACT.Copy,
                                       scale=dcol("conv_qk", 16 * it + (4 * m + 3))).then_inc(sem("cv_first"), 1)
                else:
                    for t in range(TT):
                        act.activation(v_aug[:, t, bass.ds(2 * (it - 4), 2), 0:ML_DV],
                                       ps[:, GEMM + t, :].rearrange("p (h d) -> p h d", h=2), ACT.Copy
                                       ).then_inc(sem("zv_read"), 1)
                act.wait_ge(sem("attended"), it + 1)
                act.activation(y_a[:, bass.ds(2 * it, 2), 0, :],
                               ps[:, ATT + 2, :].rearrange("p (h t) -> p h t", h=2), ACT.Copy
                               ).then_inc(sem("ya_hi"), 1)

            with act.Fori(0, 4) as j:
                mla_pass(Pos(G_MLA, j, MLA_PER), j, "qk")
            with act.Fori(0, 4) as j:
                mla_pass(Pos(G_MLA + 4 * MLA_PER, j, MLA_PER), j + 4, "v")

            def sigmoid_block(bank):
                for t in range(TT):
                    act.activation(sig[:, t, :], ps[:, bank + t, :], ACT.Sigmoid).then_inc(sem("sig_made"), 1)

            for c in range(KPB):
                split(Pos(G_ZO), c)
            act.wait_ge(sem("attended"), PAIRS)
            act.wait_ge(sem("ya_lo"), PAIRS + 1)

            def mlstm_pass(pos, j, bank):
                act.wait_ge(sem("cv_made"), 4)
                act.activation(k_st[:], qk[:, bass.ds(2 * j + ML_HEADS, 2), :], ACT.Copy).then_inc(sem("k_staged"), 1)
                sigmoid_block(bank)
                for c in range(3):
                    split(pos, c)
                act.wait_ge(sem("ml_arg"), 4 * j + 4)
                for i in range(2):
                    act.activation(w_ml[:, i, :], w_ml[:, i, :], ACT.Exp).then_inc(sem("ml_w"), 1)
                split(pos, 3)
                split(pos, 4)
                act.wait_ge(sem("ml_hn"), 4 * j + 4)
                for i in range(2):
                    for t in range(TT):
                        n = 2 * i + t
                        if n:
                            act.wait_ge(sem("ml_ss"), 4 * j + n)
                        act.activation(junk[:], hn[:, i, t, :], ACT.Square, accum_out=tiny[:, 44 + n:45 + n]
                                       ).then_inc(sem("ml_ss"), 1)
                split(pos, 5)
                act.wait_ge(sem("ml_mv"), j + 1)
                act.activation(tiny[:, 48:52], tiny[:, 48:52], ACT.Sqrt).then_inc(sem("ml_rt"), 1)
                split(pos, 6)
                split(pos, 7)
                for i in range(2):
                    act.wait_ge(sem("yb_T"), 2 * j + (i + 1))
                    for half in range(2):
                        n = 2 * i + half
                        act.activation(y_b[:, bass.ds(4 * j + n, 1), 0, :],
                                       ps[:, ATT + i, half * T:(half + 1) * T], ACT.Copy,
                                       scale=dcol("g_hnorm", 4 * j + n)).then_inc(sem("yb_hi"), 1)

            with act.Fori(0, NBLK // 2) as j:
                for n in range(2):
                    mlstm_pass(Pos(G_ML + n * KPB, j, 2 * KPB), 2 * j + n, GEMM + 2 * (1 - n))
            sigmoid_block(GEMM + 2)

            def merge_pass(pos, it, last):
                for c in range(2 * KPB):
                    split(pos, c)
                for t in range(TT):
                    act.activation(sgb[:, t, :], ps[:, GEMM + 2 + t, :], ACT.Sigmoid).then_inc(sem("sgb_made"), 1)
                for c in range(2 * KPB, 3 * KPB):
                    split(pos, c)
                if not last:
                    for c in range(3 * KPB, 3 * KPB + 4):
                        split(pos, c)
                else:
                    for c in range(3):
                        split(Pos(G_WOUT), c)
                for b in range(2):
                    act.wait_ge(sem("mg_T"), 2 * it + (b + 1))
                    act.activation(mg_t[:, bass.ds(4 * it + 2 * b, 2), 0, :],
                                   ps[:, GEMM + b, :].rearrange("p (k t) -> p k t", k=2), ACT.Copy
                                   ).then_inc(sem("mg_hi"), 1)
                if not last:
                    for c in range(3 * KPB + 4, 4 * KPB):
                        split(pos, c)
                    sigmoid_block(ATT + 2)

            with act.Fori(0, NBLK - 1) as j:
                merge_pass(Pos(G_MERGE, j, 4 * KPB), j, False)
            merge_pass(Pos(G_MERGE + 4 * KPB * (NBLK - 1)), NBLK - 1, True)

            for c in range(3, KPB):
                split(Pos(G_WOUT), c)
            norm_begin(1, mem_tok, mem_n, [(sem("mem_landed0"), 16), (sem("mem_landed1"), 16)])
            with act.Fori(0, NBLK - 2) as j:
                for c in range(KPB):
                    split(Pos(G_WOUT + KPB, j, KPB), c)
            for c in range(KPB):
                split(Pos(G_WOUT + (NBLK - 1) * KPB), c)
                norm_pair(1, mem_t, "g_mem", c)

            norm_begin(2, x_tok, xn, [(sem("x1_made"), NBLK * TT)] * 2)
            for c in range(KPB):
                split(Pos(G_CK), c)
                if c >= 4:
                    norm_pair(2, u, "g_cross", 2 * (c - 4))
                    norm_pair(2, u, "g_cross", 2 * (c - 4) + 1)

            def c_squares(n):
                for b in range(2):
                    act.activation(c_sq[:, 2 * b:2 * b + 2, :],
                                   ps[:, GEMM + 2 * n + b, :].rearrange("p (h t) -> p h t", h=2), ACT.Square
                                   ).then_inc(sem("c_sqd"), 1)

            def c_root(n):
                act.wait_ge(sem("c_mv"), 2 * n + 2)
                act.activation(c_sq[:], c_sq[:], ACT.Sqrt).then_inc(sem("c_rt"), 1)

            c_squares(0)
            for c in range(KPB):
                split(Pos(G_CQ), c)
                if c == 3:
                    c_root(0)
            act.wait_ge(sem("c_ready"), 1)
            c_squares(1)
            for c in range(KPB):
                split(Pos(G_CV), c)
                if c == 0:
                    c_root(1)
                if c == 4:
                    for h in range(CROSS_HEADS):
                        act.wait_ge(sem("c_nmax"), h + 1)
                        for t in range(TT):
                            n = 2 * h + t
                            act.activation(c_p[:, h, t, :], ps[:, ATT + h, t * T:(t + 1) * T], ACT.Exp,
                                           bias=tiny[:, 8 + n:9 + n], scale=CROSS_SCALE,
                                           accum_out=tiny[:, 16 + n:17 + n]).then_inc(sem("c_exp"), 1)
                if c == 6:
                    for h in range(CROSS_HEADS):
                        act.wait_ge(sem("c_pT"), h + 1)
                        act.activation(c_pt[:, h, :, :], ps[:, ATT + h, :].rearrange("p (s t) -> p s t", s=TT),
                                       ACT.Copy).then_inc(sem("c_pt_ready"), 1)
            for t in range(TT):
                act.activation(cv[:, t, :], ps[:, GEMM + t, :], ACT.Copy).then_inc(sem("cv_v"), 1)
            for b in range(2):
                act.wait_ge(sem("c_att"), b + 1)
                act.activation(yc[:, 2 * b:2 * b + 2, 0, :],
                               ps[:, GEMM + 2 + b, :].rearrange("p (h t) -> p h t", h=2), ACT.Copy
                               ).then_inc(sem("yc_hi"), 1)
            for n in range(NBLK + 1):
                if n < NBLK:
                    split(Pos(G_WO), 2 * n)
                if n:
                    cols_n = slice((n - 1) * BLK, n * BLK)
                    for t in range(TT):
                        act.wait_ge(sem("x2_made"), TT * (n - 1) + t + 1)
                        act.activation(xn[:, t, cols_n], x_tok[:, t, cols_n], ACT.Square,
                                       accum_out=tiny[:, 8 + NBLK * t + n - 1:8 + NBLK * t + n]
                                       ).then_inc(sem("x2_ss"), 1)
                if n < NBLK:
                    split(Pos(G_WO), 2 * n + 1)
            act.wait_ge(sem("x2_ss"), NBLK * TT)
            norm_scale(3, x_tok, xn)
            for i in range(4):
                norm_pair(3, u, "g_ffn", i)

            def up_pass(pos, j, first):
                for half, dst, pre in ((0, ua, "fa"), (1, ub, "fb")):
                    for c in range(KPB):
                        split(pos, half * KPB + c)
                        if first and half == 0 and c < 4:
                            norm_pair(3, u, "g_ffn", 4 + c)
                    for m in range(4):
                        at = 16 * j + (half * FC * 4 + 4 * m)
                        act.activation(dst[:, m, :], ps[:, GEMM + 2 * half + m // 2, (m % 2) * T:(m % 2 + 1) * T],
                                       ACT.Identity, scale=dcol("conv_ffn", at + 2), bias=dcol("conv_ffn", at + 3)
                                       ).then_inc(sem(pre + "_first"), 1)
                    if half == 0:
                        act.wait_ge(sem("fa_taps"), 8 * j + 8)
                        act.activation(ua[:], ua[:], ACT.Silu).then_inc(sem("fa_silu"), 1)

            def stage(it, kc):
                act.activation(h_st[:, kc:kc + 1, 0, :], h_ff[:, bass.ds(4 * it + kc, 1), :]
                               if not isinstance(it, int) else h_ff[:, 4 * it + kc:4 * it + kc + 1, :], ACT.Copy
                               ).then_inc(sem("hst_hi"), 1)

            up_pass(Pos(G_UP), 0, True)
            act.wait_ge(sem("h_made"), 1)
            for kc in range(4):
                stage(0, kc)
            with act.Fori(0, UP_ITER - 1) as j:
                up_pass(Pos(G_UP + UP_PER, j, UP_PER), j + 1, False)
            act.wait_ge(sem("h_made"), UP_ITER)

            def down_pass(pos, it, last):
                for c in range(DOWN_PER):
                    split(pos, c)
                    if c % 2 and not last:
                        act.wait_ge(sem("hst_lo"), 4 * it + (c // 2 + 1))
                        act.wait_ge(w_used, pos.n(c) + 1)
                        stage(it + 1, c // 2)

            with act.Fori(0, DOWN_ITER - 1) as j:
                down_pass(Pos(G_DOWN, j, DOWN_PER), j, False)
            down_pass(Pos(G_DOWN + DOWN_PER * (DOWN_ITER - 1)), DOWN_ITER - 1, True)

        @block.vector
        def _(dve):
            TTo, TS, STT = dve.tensor_tensor, dve.tensor_scalar, dve.scalar_tensor_tensor

            def split(pos, c):
                if pos.per == 0 and pos.base + c + SLOTS >= G_END:
                    return
                s = pos.slot(c)
                dve.wait_ge(hi_made, pos.n(c) + SLOTS + 1)
                TTo(w_lo[:, s, :], w_raw[:, s, :], w_hi[:, s, :].bitcast(F32), ALU.subtract).then_inc(lo_made, 1)

            def norm_begin(n, src, scratch):
                if n < 3:
                    dve.wait_ge(sem("norm_ss"), TT * (n + 1))
                else:
                    dve.wait_ge(sem("x2_ss"), NBLK * TT)
                    dve.tensor_reduce(tiny[:, 0:2], tiny[:, 8:8 + NBLK * TT].rearrange("p (t n) -> p t n", t=TT),
                                      AX_X, ALU.add).then_inc(sem("x2_sum"), 1)
                    dve.wait_ge(sem("x2_sum"), 1)
                TS(tiny[:, 2:4], tiny[:, 0:2], 1.0 / D, EPS, ALU.mult, ALU.add).then_inc(sem("norm_mv"), 1)
                dve.wait_ge(sem("norm_rt"), n + 1)
                dve.reciprocal(tiny[:, 6:8], tiny[:, 4:6]).then_inc(sem("norm_r"), 1)
                dve.wait_ge(sem("norm_r"), n + 1)
                TS(scratch[:, 0, :], src[:, 0, :], tiny[:, 6:7], None, ALU.mult).then_inc(sem("norm_xn0"), 1)

            def norm_pair(n, dst, gain, i):
                dve.wait_ge(sem("norm_hi"), KC * n + 2 * i + 2)
                for k in range(2):
                    kc = 2 * i + k
                    STT(dst[:, kc, 1, :], ps[:, ATT + i % 4, k * T:(k + 1) * T], col(gain, kc),
                        dst[:, kc, 0, :].bitcast(F32), ALU.mult, ALU.subtract).then_inc(sem("norm_lo"), 1)

            dve.memset(ones8[:], 1.0).then_inc(sem("ones"), 1)
            dve.memset(q_early[:], 0.0).then_inc(sem("ones"), 1)
            dve.memset(k_late[:], 0.0).then_inc(sem("ones"), 1)
            dve.wait_ge(sem("ones"), 3)
            dve.memset(q_early[:, 0:CHUNK], 1.0).then_inc(sem("ones"), 1)
            dve.memset(k_late[:, CHUNK:2 * CHUNK], -1e30).then_inc(sem("ones"), 1)

            norm_begin(0, x0_tok, x0_n)
            for g in range(SLOTS):
                dve.wait_ge(hi_made, g + 1)
                TTo(w_lo[:, g, :], w_raw[:, g, :], w_hi[:, g, :].bitcast(F32), ALU.subtract).then_inc(lo_made, 1)
                if g == 0:
                    for i in range(KC // 2):
                        norm_pair(0, u, "g_mix", i)

            n = 0

            def step(ins):
                nonlocal n
                n += 1
                ins.then_inc(sem("rope_step"), 1)
                dve.wait_ge(sem("rope_step"), n)

            TWO_PI = 2 * np.pi
            c1 = 6.28125
            c2 = float(np.floor((TWO_PI - c1) * 2 ** 20) / 2 ** 20)
            c3 = float(TWO_PI - c1 - c2)
            BIG = 1.5 * 2.0 ** 23
            PI_IN = 3.1415925
            dve.wait_ge(sem("pos_landed"), 16)
            dve.wait_ge(sem("cols_landed"), 16)
            step(dve.tensor_copy(gq[:, 1, :], gq[:, 0, :].bitcast(I32)))
            step(TS(gq[:, 1, :], gq[:, 1, :], col("inv_freq"), None, ALU.mult))
            step(TS(gp[:], gq[:, 1, :], float(1.0 / TWO_PI), BIG, ALU.mult, ALU.add))
            step(TS(gp[:], gp[:], BIG, None, ALU.subtract))
            step(STT(gk[:, 0, :], gp[:], -c1, gq[:, 1, :], ALU.mult, ALU.add))
            step(STT(gk[:, 0, :], gp[:], -c2, gk[:, 0, :], ALU.mult, ALU.add))
            step(STT(gk[:, 0, :], gp[:], -c3, gk[:, 0, :], ALU.mult, ALU.add))
            step(TS(gp[:], gk[:, 0, :], float(np.pi / 2), -TWO_PI, ALU.is_gt, ALU.mult))
            step(STT(gk[:, 1, :], gk[:, 0, :], float(np.pi / 2), gp[:], ALU.add, ALU.add))
            step(TS(gk[:, 1, :], gk[:, 1, :], -PI_IN, PI_IN, ALU.max, ALU.min))
            TS(gk[:, 0, :], gk[:, 0, :], -PI_IN, PI_IN, ALU.max, ALU.min).then_inc(sem("angles"), 1)

            pos = Pos(0)
            for c in range(N_NARROW):
                split(pos, c)
            dve.wait_ge(sem("kpx_made"), 2)
            TS(kpx[:, 1, :], kpx[:, 2, :], col("g_kn_pe", 0, slice(0, ROPE)), None, ALU.mult
               ).then_inc(sem("kpg_made"), 1)
            dve.wait_ge(sem("z8"), 2)
            TS(zf8[:], zf8[:], col("b_f", 0, slice(0, 8)), None, ALU.add).then_inc(sem("f_made"), 1)
            TS(zi8[:], zi8[:], col("b_i", 0, slice(0, 8)), None, ALU.add).then_inc(sem("i_made"), 1)
            for c in range(KPB):
                split(pos, G_QA + c)
                if c == 0:
                    dve.wait_ge(sem("ls_act"), 2)
                    TS(g8b[:], g8b[:], 1.0, None, ALU.add).then_inc(sem("e_plus"), 1)
                    TS(zf8[:], zf8[:], 0.0, None, ALU.min).then_inc(sem("f_min"), 1)
                if c == 2:
                    dve.wait_ge(sem("ls_act"), 3)
                    dve.wait_ge(sem("f_min"), 1)
                    TTo(zf8[:], zf8[:], g8a[:], ALU.subtract).then_inc(sem("gate"), 1)
                    dve.memset(g8b[:], 0.0).then_inc(sem("gate"), 1)
                    dve.wait_ge(sem("gate"), 2)
                    dve.tensor_tensor_scan(g8a[:], zf8[:], g8b[:], 0.0, ALU.add, ALU.add).then_inc(sem("gate"), 1)
                    dve.wait_ge(sem("gate"), 3)
                    TTo(zi8[:], zi8[:], g8a[:], ALU.subtract).then_inc(sem("gate"), 1)
                    dve.wait_ge(sem("gate"), 4)
                    dve.tensor_tensor_scan(ncm[:], zi8[:], zi8[:], 0.0, ALU.max, ALU.max).then_inc(sem("gate"), 1)
                    dve.wait_ge(sem("gate"), 5)
                    TTo(g8b[:], g8a[:], ncm[:], ALU.add).then_inc(sem("m_neg"), 1)
                    dve.wait_ge(sem("m_neg"), 1)
                    TS(ncm[:], ncm[:], -1.0, None, ALU.mult).then_inc(sem("gate"), 1)
                    dve.tensor_copy(g8a[:], zi8[:]).then_inc(sem("gate"), 1)
                    dve.wait_ge(sem("gate"), 7)
                if c == 3:
                    dve.wait_ge(sem("kp_rot"), 1)
                    dve.wait_ge(sem("tables"), 2)
                    TS(kpx[:, 0, :], ps[0:ROPE, ATT + 1, 0:T], EPS, None, ALU.add).then_inc(sem("kp_mv"), 1)
                    TTo(kpx[:, 2, :], ps[0:ROPE, ATT + 1, T:2 * T], sin_t[0:ROPE, :], ALU.mult
                        ).then_inc(sem("kp"), 1)
                    TTo(kpx[:, 1, :], kpx[:, 1, :], cos_t[0:ROPE, :], ALU.mult).then_inc(sem("kp"), 1)
                    dve.wait_ge(sem("kp"), 2)
                    TTo(kpx[:, 1, :], kpx[:, 1, :], kpx[:, 2, :], ALU.add).then_inc(sem("kp"), 1)
                    dve.wait_ge(sem("kp_rt"), 1)
                    dve.reciprocal(kpx[:, 0, :], kpx[:, 0, :]).then_inc(sem("kp"), 1)
                    dve.wait_ge(sem("kp"), 4)
                    TTo(kpe[0:ROPE, :], kpx[:, 1, :], kpx[:, 0, :], ALU.mult).then_inc(sem("kpe_made"), 1)

            def latent(i):
                dve.wait_ge(sem("lat_ss"), TT * (i + 1))
                TS(tiny[:, 12 + 2 * i:14 + 2 * i], tiny[:, 8 + 2 * i:10 + 2 * i], 1.0 / LORA, EPS, ALU.mult, ALU.add
                   ).then_inc(sem("lat_mv"), 1)
                dve.wait_ge(sem("lat_rt"), i + 1)
                dve.reciprocal(tiny[:, 20 + 2 * i:22 + 2 * i], tiny[:, 16 + 2 * i:18 + 2 * i]
                               ).then_inc(sem("lat_r"), 1)

            def latent_lo(i, dst, gain):
                for b in range(2):
                    dve.wait_ge(sem("lat_hi"), 4 * i + 2 * b + 2)
                    for k in range(2):
                        kc = 2 * b + k
                        STT(dst[:, kc, 1, :], ps[:, ATT + 2 + b, k * T:(k + 1) * T], col(gain, kc),
                            dst[:, kc, 0, :].bitcast(F32), ALU.mult, ALU.subtract).then_inc(sem("lat_lo"), 1)

            latent(0)
            for c in range(KPB):
                split(pos, G_KV + c)
                if c == 5:
                    latent_lo(0, qa_t, "g_qa")
            latent(1)
            latent_lo(1, kv_t, "g_kva")
            dve.memset(v_aug[:, :, :, ML_DV:DV1], 1.0).then_inc(sem("ya_lo"), 1)

            def mla_pass(pos, it, filler):
                split(pos, 0)
                split(pos, 1)
                dve.wait_ge(sem("sqq_made"), it + 1)
                TS(gq[:].rearrange("p h t -> p (h t)"), ps[:, ATT, :], col("g_qn_nope"), None, ALU.mult
                   ).then_inc(sem("gq_made"), 1)
                dve.wait_ge(sem("sqp_made"), it + 1)
                TS(gp[:], ps[:, ATT + 3, 0:T], col("g_qn_pe"), None, ALU.mult).then_inc(sem("gp_made"), 1)
                split(pos, 2)
                split(pos, 3)
                dve.wait_ge(sem("sqk_made"), it + 1)
                TS(gk[:].rearrange("p h t -> p (h t)"), ps[:, ATT + 1, :], col("g_kn_nope"), None, ALU.mult
                   ).then_inc(sem("gk_made"), 1)
                fq, fk = (b[:].rearrange("p h t -> p (h t)") for b in (gq, gk))
                yq, yk = (b[:].rearrange("p h t -> p (h t)") for b in (sq_q, sq_k))
                inv, rp, n = sem("inv_rms"), sem("rp"), 11 * it
                dve.wait_ge(sem("ms_p"), it + 1)
                TTo(gp[:], gp[:], cos_t[:], ALU.mult).then_inc(rp, 1)
                dve.wait_ge(inv, 9 * it + 2)
                TTo(rope_2, ps[:, ATT + 3, T:2 * T], sin_t[:], ALU.mult).then_inc(rp, 1)
                dve.wait_ge(inv, 9 * it + 5)
                STT(y2_q, ps[:, ATT, :], EPS, y2_q, ALU.add, ALU.mult).then_inc(rp, 1)
                TTo(fq, fq, yq, ALU.mult).then_inc(rp, 1)
                split(pos, 4)
                dve.wait_ge(rp, n + 2)
                STT(gp[:], rope_2, -1.0, gp[:], ALU.mult, ALU.subtract).then_inc(rp, 1)
                dve.wait_ge(inv, 9 * it + 6)
                STT(y2_p, ps[:, ATT + 3, 0:T], EPS, y2_p, ALU.add, ALU.mult).then_inc(rp, 1)
                dve.wait_ge(rp, n + 5)
                TTo(gp[:], gp[:], sq_p[:], ALU.mult).then_inc(rp, 1)
                STT(fq, y2_q, -1.5, fq, ALU.add, ALU.mult).then_inc(rp, 1)
                dve.wait_ge(rp, n + 7)
                STT(gp[:], y2_p, -1.5, gp[:], ALU.add, ALU.mult).then_inc(rp, 1)
                split(pos, 5)
                dve.wait_ge(inv, 9 * it + 9)
                STT(y2_k, ps[:, ATT + 1, :], EPS, y2_k, ALU.add, ALU.mult).then_inc(rp, 1)
                TTo(fk, fk, yk, ALU.mult).then_inc(rp, 1)
                dve.wait_ge(rp, n + 11)
                STT(fk, y2_k, -1.5, fk, ALU.add, ALU.mult).then_inc(sem("qk_ready"), 1)
                split(pos, 6)
                split(pos, 7)
                for h in range(2):
                    dve.wait_ge(sem("scored"), 2 * it + (h + 1))
                    for t in range(TT):
                        k = 2 * h + t
                        dve.tensor_reduce(tiny[:, 24 + k:25 + k], ps[:, ATT + h, t * P:t * P + (t + 1) * P], AX_X,
                                          ALU.max).then_inc(sem("row_max"), 1)
                dve.wait_ge(sem("row_max"), 4 * it + 4)
                TS(tiny[:, 28:32], tiny[:, 24:28], -MLA_SCALE, None, ALU.mult).then_inc(sem("neg_max"), 1)
                dve.wait_ge(sem("p_exp"), 4 * it + 4)
                dve.reciprocal(tiny[:, 36:40], tiny[:, 32:36]).then_inc(sem("p_rs"), 1)
                dve.wait_ge(sem("p_rs"), it + 1)
                for h in range(2):
                    for t in range(TT):
                        k = 2 * h + t
                        ins = TS(pr[:, h, t * P:t * P + (t + 1) * P], pr[:, h, t * P:t * P + (t + 1) * P],
                                 tiny[:, 36 + k:37 + k], None, ALU.mult)
                ins.then_inc(sem("p_ready"), 1)
                split(pos, 8)
                split(pos, 9)
                dve.wait_ge(sem("pT"), 2 * it + 2)
                dve.wait_ge(sem("pt_1"), it + 1)
                dve.tensor_copy(prt[:, 0, :], ps[:, ATT, 0:384]).then_inc(sem("pt_ready"), 2)
                split(pos, 10)
                split(pos, 11)
                dve.wait_ge(sem("ya_hi"), it + 1)
                TTo(y_a[:, bass.ds(2 * it, 2), 1, :], ps[:, ATT + 2, :].rearrange("p (h t) -> p h t", h=2),
                    y_a[:, bass.ds(2 * it, 2), 0, :].bitcast(F32), ALU.subtract).then_inc(sem("ya_lo"), 1)
                if filler == "qk":
                    dve.wait_ge(sem("cv_first"), 4 * it + 4)
                    for tap in (2, 1, 0):
                        lag = 3 - tap
                        if tap < 2:
                            dve.wait_ge(sem("cv_taps"), 12 * it + 4 * (2 - tap))
                        for m in range(4):
                            dst = qk[:, bass.ds(4 * it + m, 1), lag:T].rearrange("p o t -> p (o t)")
                            STT(dst, ps[:, GEMM + m // 2, (m % 2) * T:(m % 2 + 1) * T - lag],
                                dcol("conv_qk", 16 * it + (4 * m + tap)), dst, ALU.mult, ALU.add
                                ).then_inc(sem("cv_taps"), 1)

            with dve.Fori(0, 4) as j:
                mla_pass(Pos(G_MLA, j, MLA_PER), j, "qk")
            with dve.Fori(0, 4) as j:
                mla_pass(Pos(G_MLA + 4 * MLA_PER, j, MLA_PER), j + 4, "v")

            for c in range(KPB):
                split(Pos(G_ZO), c)

            dve.wait_ge(sem("attended"), PAIRS)
            def mlstm_pass(pos, j):
                for i in range(2):
                    TS(m_st[:, i, :], ncm[:], mats[0:8, bass.ds(2 * j + i, 1)], None, ALU.mult
                       ).then_inc(sem("m_staged"), 1)
                split(pos, 0)
                split(pos, 1)
                dve.wait_ge(sem("ml_scored"), j + 1)
                for i in range(2):
                    TS(w_ml[:, i, 0:T], ps[:, ATT + 2, i * T:(i + 1) * T],
                       a_tok[:, 0, bass.ds(2 * j + i, 1)], 0.0, ALU.add, ALU.min).then_inc(sem("ml_arg"), 1)
                    TS(w_ml[:, i, T:T + P], ps[:, ATT + 2, i * T + P:(i + 1) * T],
                       a_tok[:, 1, bass.ds(2 * j + i, 1)], 0.0, ALU.add, ALU.min).then_inc(sem("ml_arg"), 1)
                split(pos, 2)
                for i in range(2):
                    dve.wait_ge(sem("ml_w"), 2 * j + (i + 1))
                    for d in (0, T):
                        TTo(w_ml[:, i, d:d + P], w_ml[:, i, d:d + P], tri, ALU.mult).then_inc(sem("ml_tri"), 1)
                for i in range(2):
                    dve.wait_ge(sem("ml_tri"), 4 * j + 2 * (i + 1))
                    STT(w_ml[:, i, :], ps[:, ATT + i, 0:384], ML_SCALE, w_ml[:, i, :], ALU.mult, ALU.mult
                        ).then_inc(sem("ml_p"), 1)
                split(pos, 3)
                split(pos, 4)
                dve.wait_ge(sem("ml_num"), j + 1)
                for k in range(4):
                    dve.tensor_copy(tiny[:, 40 + k:41 + k], ps[:, ATT + k, ML_DV:DV1]).then_inc(sem("ml_den"), 1)
                dve.wait_ge(sem("ml_den"), 6 * j + 4)
                STT(tiny[:, 56:60], tiny[:, 40:44], -1.0, tiny[:, 40:44], ALU.mult, ALU.max
                    ).then_inc(sem("ml_den"), 1)
                dve.wait_ge(sem("ml_den"), 6 * j + 5)
                TTo(tiny[:, 40:44].rearrange("p (i t) -> p i t", t=TT),
                    tiny[:, 56:60].rearrange("p (i t) -> p i t", t=TT),
                    e_tok[:, :, bass.ds(2 * j, 2)].rearrange("p t i -> p i t"), ALU.max).then_inc(sem("ml_den"), 1)
                dve.wait_ge(sem("ml_den"), 6 * j + 6)
                dve.reciprocal(tiny[:, 40:44], tiny[:, 40:44]).then_inc(sem("ml_rd"), 1)
                dve.wait_ge(sem("ml_rd"), j + 1)
                for i in range(2):
                    for t in range(TT):
                        k = 2 * i + t
                        TS(hn[:, i, t, :], ps[:, ATT + k, 0:ML_DV], tiny[:, 40 + k:41 + k], None, ALU.mult
                           ).then_inc(sem("ml_hn"), 1)
                split(pos, 5)
                dve.wait_ge(sem("ml_ss"), 4 * j + 4)
                TS(tiny[:, 48:52], tiny[:, 44:48], 1.0 / ML_DV, EPS, ALU.mult, ALU.add).then_inc(sem("ml_mv"), 1)
                dve.wait_ge(sem("ml_rt"), j + 1)
                dve.reciprocal(tiny[:, 52:56], tiny[:, 48:52]).then_inc(sem("ml_rr"), 1)
                dve.wait_ge(sem("ml_rr"), j + 1)
                dve.wait_ge(sem("sig_made"), TT * j + TT)
                for i in range(2):
                    for t in range(TT):
                        k = 2 * i + t
                        STT(hn[:, i, t, :], hn[:, i, t, :], tiny[:, 52 + k:53 + k],
                            sig[:, t, i * ML_DV:(i + 1) * ML_DV], ALU.mult, ALU.mult).then_inc(sem("yb_tok"), 1)
                split(pos, 6)
                split(pos, 7)
                for i in range(2):
                    dve.wait_ge(sem("yb_hi"), 4 * j + 2 * (i + 1))
                    for half in range(2):
                        k = 2 * i + half
                        STT(y_b[:, bass.ds(4 * j + k, 1), 1, :].rearrange("p o t -> p (o t)"),
                            ps[:, ATT + i, half * T:(half + 1) * T], dcol("g_hnorm", 4 * j + k),
                            y_b[:, bass.ds(4 * j + k, 1), 0, :].bitcast(F32).rearrange("p o t -> p (o t)"),
                            ALU.mult, ALU.subtract).then_inc(sem("yb_lo"), 1)

            with dve.Fori(0, NBLK // 2) as j:
                for n in range(2):
                    mlstm_pass(Pos(G_ML + n * KPB, j, 2 * KPB), 2 * j + n)

            def merge_pass(pos, it, last):
                for c in range(KPB):
                    split(pos, c)
                dve.wait_ge(sem("sig_made"), TT * (NBLK + 1) + TT * it)
                for t in range(TT):
                    TTo(mg_a[:, t, :], ps[:, GEMM + t, :], sig[:, t, :], ALU.mult).then_inc(sem("mga"), 1)
                for c in range(KPB, 3 * KPB):
                    split(pos, c)
                dve.wait_ge(sem("sgb_made"), TT * it + TT)
                for t in range(TT):
                    TTo(mg[:, t, :], ps[:, ATT + t, :], sgb[:, t, :], ALU.mult).then_inc(sem("mgb_read"), 1)
                dve.wait_ge(sem("mgb_read"), TT * it + TT)
                dve.wait_ge(sem("mga"), TT * it + TT)
                TTo(mg[:], mg[:], mg_a[:], ALU.add).then_inc(sem("mg_made"), 1)
                if not last:
                    for c in range(3 * KPB, 3 * KPB + 4):
                        split(pos, c)
                else:
                    for c in range(3):
                        split(Pos(G_WOUT), c)
                for b in range(2):
                    dve.wait_ge(sem("mg_hi"), 2 * it + (b + 1))
                    TTo(mg_t[:, bass.ds(4 * it + 2 * b, 2), 1, :],
                        ps[:, GEMM + b, :].rearrange("p (k t) -> p k t", k=2),
                        mg_t[:, bass.ds(4 * it + 2 * b, 2), 0, :].bitcast(F32), ALU.subtract
                        ).then_inc(sem("mg_lo"), 1)
                if not last:
                    for c in range(3 * KPB + 4, 4 * KPB):
                        split(pos, c)

            with dve.Fori(0, NBLK - 1) as j:
                merge_pass(Pos(G_MERGE, j, 4 * KPB), j, False)
            merge_pass(Pos(G_MERGE + 4 * KPB * (NBLK - 1)), NBLK - 1, True)

            def wout_block(pos, it, bank):
                for c in range(3 if it == 0 else 0, KPB):
                    split(pos, c)
                    if it == NBLK - 1:
                        norm_pair(1, mem_t, "g_mem", c)
                dve.wait_ge(w_used, pos.n(KPB))
                for t in range(TT):
                    xs = (x_tok[:, t, it * BLK:(it + 1) * BLK] if isinstance(it, int)
                          else x_tok[:, t, bass.ds(it * BLK, BLK)])
                    TTo(xs, ps[:, bank + t, :], xs, ALU.add).then_inc(sem("x1_made"), 1)

            dve.wait_ge(sem("x_again0"), 16)
            dve.wait_ge(sem("x_again1"), 16)
            wout_block(Pos(G_WOUT), 0, GEMM + 2)
            norm_begin(1, mem_tok, mem_n)
            for n in range(1, NBLK):
                wout_block(Pos(G_WOUT + n * KPB), n, GEMM + 2 * (1 - n % 2))
            norm_begin(2, x_tok, xn)
            for c in range(KPB):
                split(Pos(G_CK), c)
                if c >= 4:
                    norm_pair(2, u, "g_cross", 2 * (c - 4))
                    norm_pair(2, u, "g_cross", 2 * (c - 4) + 1)

            def c_gain(n, dst, gain):
                dve.wait_ge(sem("c_sqd"), 2 * n + 2)
                for b in range(2):
                    ins = TS(dst[:, 2 * b:2 * b + 2, :], ps[:, GEMM + 2 * n + b, :].rearrange("p (h t) -> p h t", h=2),
                             col(gain), None, ALU.mult)
                ins.then_inc(sem("c_g"), 1)

            def c_norm(n, dst, pos, c):
                dve.wait_ge(sem("c_ms"), n + 1)
                for b in range(2):
                    TS(c_sq[:, 2 * b:2 * b + 2, :], ps[:, ATT + b, :].rearrange("p (h t) -> p h t", h=2), EPS, None,
                       ALU.add).then_inc(sem("c_mv"), 1)
                dve.wait_ge(sem("c_rt"), n + 1)
                for b in range(2):
                    half = c_sq[:, 2 * b:2 * b + 2, :]
                    dve.reciprocal(half, half).then_inc(sem("c_rc"), 1)
                    if b == 0:
                        split(pos, c)
                dve.wait_ge(sem("c_rc"), 2 * n + 2)
                dve.wait_ge(sem("c_g"), n + 1)
                TTo(dst[:], dst[:], c_sq[:], ALU.mult).then_inc(sem("c_ready"), 1)

            c_gain(0, ck, "g_ck")
            for c in range(4):
                split(Pos(G_CQ), c)
            c_norm(0, ck, Pos(G_CQ), 4)
            for c in range(5, KPB):
                split(Pos(G_CQ), c)
            c_gain(1, cq, "g_cq")
            split(Pos(G_CV), 0)
            c_norm(1, cq, Pos(G_CV), 1)
            for c in (2, 3, 4):
                split(Pos(G_CV), c)
            for h in range(CROSS_HEADS):
                dve.wait_ge(sem("c_scored"), h + 1)
                dve.tensor_reduce(tiny[:, 24 + 2 * h:26 + 2 * h],
                                  ps[:, ATT + h, :].rearrange("p (t k) -> p t k", t=TT), AX_X, ALU.max
                                  ).then_inc(sem("c_max"), 1)
                dve.wait_ge(sem("c_max"), h + 1)
                TS(tiny[:, 8 + 2 * h:10 + 2 * h], tiny[:, 24 + 2 * h:26 + 2 * h], -CROSS_SCALE, None, ALU.mult
                   ).then_inc(sem("c_nmax"), 1)
            split(Pos(G_CV), 5)
            for h in range(CROSS_HEADS):
                dve.wait_ge(sem("c_exp"), 2 * h + 2)
                dve.reciprocal(tiny[:, 32 + 2 * h:34 + 2 * h], tiny[:, 16 + 2 * h:18 + 2 * h]
                               ).then_inc(sem("c_rs"), 1)
                dve.wait_ge(sem("c_rs"), h + 1)
                for t in range(TT):
                    k = 32 + 2 * h + t
                    ins = TS(c_p[:, h, t, :], c_p[:, h, t, :], tiny[:, k:k + 1], None, ALU.mult)
                ins.then_inc(sem("c_p_ready"), 1)
            split(Pos(G_CV), 6)
            split(Pos(G_CV), 7)
            for b in range(2):
                dve.wait_ge(sem("yc_hi"), b + 1)
                TTo(yc[:, 2 * b:2 * b + 2, 1, :], ps[:, GEMM + 2 + b, :].rearrange("p (h t) -> p h t", h=2),
                    yc[:, 2 * b:2 * b + 2, 0, :].bitcast(F32), ALU.subtract).then_inc(sem("yc_lo"), 1)
            for n in range(NBLK):
                for c in range(2):
                    split(Pos(G_WO), 2 * n + c)
                dve.wait_ge(w_used, G_WO + 2 * n + 2)
                for t in range(TT):
                    xs = x_tok[:, t, n * BLK:(n + 1) * BLK]
                    TTo(xs, ps[:, 2 * n + t, :], xs, ALU.add).then_inc(sem("x2_made"), 1)
            norm_begin(3, x_tok, xn)
            for i in range(4):
                norm_pair(3, u, "g_ffn", i)

            def up_pass(pos, j, first):
                rows = bass.ds(4 * j, 4) if not isinstance(j, int) else slice(4 * j, 4 * j + 4)
                for half, dst, pre in ((0, ua, "fa"), (1, ub, "fb")):
                    for c in range(KPB):
                        split(pos, half * KPB + c)
                        if first and half == 0 and c < 4:
                            norm_pair(3, u, "g_ffn", 4 + c)
                    dve.wait_ge(sem(pre + "_first"), 4 * j + 4)
                    for tap in (1, 0):
                        lag = 2 - tap
                        if tap == 0:
                            dve.wait_ge(sem(pre + "_taps"), 8 * j + 4)
                        for m in range(4):
                            STT(dst[:, m, lag:T], ps[:, GEMM + 2 * half + m // 2, (m % 2) * T:(m % 2 + 1) * T - lag],
                                dcol("conv_ffn", 16 * j + (half * FC * 4 + 4 * m + tap)), dst[:, m, lag:T],
                                ALU.mult, ALU.add).then_inc(sem(pre + "_taps"), 1)
                dve.wait_ge(sem("fb_taps"), 8 * j + 8)
                dve.wait_ge(sem("fa_silu"), j + 1)
                TTo(h_ff[:, rows, :], ua[:], ub[:], ALU.mult).then_inc(sem("h_made"), 1)

            def stage(it, kc):
                src = (h_ff[:, 4 * it + kc:4 * it + kc + 1, :] if isinstance(it, int)
                       else h_ff[:, bass.ds(4 * it + kc, 1), :])
                dve.wait_ge(sem("hst_hi"), 4 * it + (kc + 1))
                TTo(h_st[:, kc:kc + 1, 1, :], src, h_st[:, kc:kc + 1, 0, :].bitcast(F32), ALU.subtract
                    ).then_inc(sem("hst_lo"), 1)

            up_pass(Pos(G_UP), 0, True)
            dve.wait_ge(sem("h_made"), 1)
            for kc in range(4):
                stage(0, kc)
            with dve.Fori(0, UP_ITER - 1) as j:
                up_pass(Pos(G_UP + UP_PER, j, UP_PER), j + 1, False)
            dve.wait_ge(sem("h_made"), UP_ITER)

            def down_pass(pos, it, last):
                for c in range(DOWN_PER):
                    split(pos, c)
                    if c % 2 and not last:
                        stage(it + 1, c // 2)

            with dve.Fori(0, DOWN_ITER - 1) as j:
                down_pass(Pos(G_DOWN, j, DOWN_PER), j, False)
            down_pass(Pos(G_DOWN + DOWN_PER * (DOWN_ITER - 1)), DOWN_ITER - 1, True)
            for n in range(NBLK):
                dve.wait_ge(w_used, G_END - 1 + n // 2)
                for t in range(TT):
                    xs = x_tok[:, t, n * BLK:(n + 1) * BLK]
                    TTo(xs, ps[:, t * 4 + n, :], xs, ALU.add).then_inc(sem("out_made"), 1)


def lay_out(i):
    f = np.float32
    w_in = np.asarray(i["w_in"])[0]
    at = np.cumsum([0, 512, 512, 64, 1024, 1024, 2048, 8, 8, 2048, 2048, 2048])
    qa0, kv0, kp0, q0, k0, v0, i0, f0, o0, ga0, gb0 = (int(a) for a in at[:-1])
    chunks = []

    def block(w, n0, width=BLK, rows=None):
        kk = w.shape[0] // P
        b = w[:, n0:n0 + width].reshape(kk // 2, 2, P, width).transpose(0, 2, 1, 3)
        chunks.append(b.reshape(kk // 2, P, 2 * width))

    narrow = np.zeros((D, P), f)
    narrow[:, 0:64] = w_in[:, kp0:kp0 + 64]
    narrow[:, 64:72] = w_in[:, i0:i0 + 8]
    narrow[:, 96:104] = w_in[:, f0:f0 + 8]
    chunks.append(narrow.reshape(2, 8, P, P).transpose(0, 2, 1, 3).reshape(2, P, 1024))
    block(w_in, qa0)
    block(w_in, kv0)
    wq = np.asarray(i["w_qb"])[0].reshape(LORA, PAIRS, 2, NOPE + ROPE)
    wkv = np.asarray(i["w_kvb"])[0].reshape(LORA, PAIRS, 2, 2, P)
    fill = [q0, q0 + BLK, k0, k0 + BLK] + [v0 + n * BLK for n in range(4)]
    for pair in range(PAIRS):
        b = np.zeros((LORA, BLK), f)
        b[:, 0:256] = wq[:, pair, :, 0:NOPE].reshape(LORA, 256)
        b[:, 256:384] = wq[:, pair, :, NOPE:].reshape(LORA, 128)
        block(b, 0)
        block(wkv[:, pair].transpose(0, 2, 1, 3).reshape(LORA, BLK), 0)
        block(w_in, fill[pair])
    for n in range(4):
        block(w_in, o0 + n * BLK)
    block(w_in, ga0)
    p_a, p_b, w_out = (np.asarray(i[n])[0] for n in ("p_a", "p_b", "w_out"))
    for n in range(4):
        block(p_a, n * BLK)
        block(w_in, gb0 + n * BLK)
        block(p_b, n * BLK)
        if n < 3:
            block(w_in, ga0 + (n + 1) * BLK)
    for n in range(4):
        block(w_out, n * BLK)
    for name in ("wk_c", "wq_c", "wv_c"):
        block(np.asarray(i[name])[0], 0)
    wo = np.asarray(i["wo_c"])[0]
    for n in range(4):
        block(wo, n * BLK)
    w_up = np.asarray(i["w_up"])[0]
    for n in range(UP_ITER):
        block(w_up, n * BLK)
        block(w_up, D_FF + n * BLK)
    w_down = np.asarray(i["w_down"])[0]
    chunks.append(w_down.reshape(FC, P, 2, 1024).transpose(0, 2, 1, 3).reshape(2 * FC, P, 1024))
    stream = np.concatenate(chunks)
    assert stream.shape[0] == G_END

    cols = np.zeros((P, NCOLS), f)

    def put(name, v, n=1):
        cols[:v.shape[0], COLS[name]:COLS[name] + n] = v.reshape(v.shape[0], n)

    for name in ("g_mix", "g_mem", "g_cross", "g_ffn"):
        put(name, np.asarray(i[name])[0].reshape(KC, P).T, KC)
    put("g_hnorm", np.asarray(i["g_hnorm"])[0].reshape(KC, P).T, KC)
    for name in ("g_qa", "g_kva"):
        put(name, np.asarray(i[name])[0].reshape(LC, P).T, LC)
    for name in ("g_qn_nope", "g_kn_nope", "g_cq", "g_ck"):
        put(name, np.asarray(i[name])[0])
    for name in ("g_qn_pe", "g_kn_pe"):
        put(name, np.tile(np.asarray(i[name])[0], 2))
    inv = f(ROPE_BASE) ** (-np.arange(0, ROPE, 2, dtype=f) / f(ROPE))
    put("inv_freq", np.tile(inv.astype(f), 4))
    put("b_i", np.asarray(i["b_if"])[0][0:8])
    put("b_f", np.asarray(i["b_if"])[0][8:16])
    put("conv_qk", np.asarray(i["conv_qk"])[0].reshape(4, 16, P).transpose(2, 1, 0), 64)
    ffn = np.zeros((P, 2 * FC, 4), f)
    ffn[:, :, 0:3] = np.asarray(i["conv_ffn"])[0].reshape(3, 2 * FC, P).transpose(2, 1, 0)
    ffn[:, :, 3] = np.asarray(i["b_conv_ffn"])[0].reshape(2 * FC, P).T
    put("conv_ffn", ffn, 2 * FC * 4)
    put("eps", np.full((P,), EPS, f))

    mats = np.zeros((P, 5 * P), f)
    mats[:, 0:P] = np.eye(P)
    for h in range(2):
        for a in range(ROPE // 2):
            lo, hi = h * ROPE + a, h * ROPE + a + ROPE // 2
            mats[hi, P + lo] = -1.0
            mats[lo, P + hi] = 1.0
    mats[:, 2 * P:3 * P] = 1.0 / P
    for h in range(2):
        mats[h * ROPE:(h + 1) * ROPE, 3 * P + h * ROPE:3 * P + (h + 1) * ROPE] = 1.0 / ROPE
    mats[:, 4 * P:5 * P] = np.triu(np.ones((P, P), f))
    return {
        "x": np.asarray(i["x"])[0], "mem": np.asarray(i["mem"])[0], "positions": np.asarray(i["positions"])[0],
        "cols": cols, "mats": mats, "stream": stream,
    }


def kernel(**inputs):
    import concourse.bacc as bacc
    from concourse.bass_utils import run_bass_kernel_spmd

    nc = bacc.Bacc("TRN2", target_bir_lowering=False, num_devices=1)
    arrays, args = {}, []
    for name, a in lay_out(inputs).items():
        a = np.ascontiguousarray(a)
        arrays[f"in_{name}"] = a
        args.append(nc.dram_tensor(f"in_{name}", a.shape, mybir.dt.from_np(a.dtype), kind="ExternalInput").ap())
    out = nc.dram_tensor("out", (T, D), F32, kind="ExternalOutput").ap()
    build(nc, *args, out)
    r = run_bass_kernel_spmd(nc, [arrays], core_ids=[0])
    return np.asarray(r.results[0]["out"]).reshape(1, T, D)
```
